# Optimizing a Trainium2 kernel written in Bass

```python
import jax, jax.numpy as jnp
from jax import lax
import numpy as np

D_MODEL = 2048
BATCH = 1
SEQ = 512
DEPTH = 1

CHUNK = 64
HEAD_DIM = 64
EPS = 1e-5
A_Q_HEADS = 16
A_KV_HEADS = 4
A_GROUP = A_Q_HEADS // A_KV_HEADS
A_WINDOW = 128
A_PREV_CHUNKS = A_WINDOW // CHUNK - 1
A_WIDTH = A_Q_HEADS * HEAD_DIM
A_KV_WIDTH = A_KV_HEADS * HEAD_DIM
B_HEADS = 16
B_PREV_CHUNKS = 8
B_REL_CLIP = 256
B_WIDTH = B_HEADS * HEAD_DIM
IN_WIDTH = A_WIDTH + 2 * A_KV_WIDTH + 3 * B_WIDTH
D_FF = 4 * D_MODEL
NEG_INF = -1e30

kernel_name = "gated_chunk_hybrid_swa_relbias_encoder"

def rms_norm(x, g):
    xf = x.astype(jnp.float32)
    y = xf * lax.rsqrt(jnp.mean(xf * xf, axis=-1, keepdims=True) + EPS)
    return (y * g.astype(jnp.float32)).astype(x.dtype)

def gather_band(k, n_prev):
    b, s, h, d = k.shape
    nc = s // CHUNK
    kc = k.reshape(b, nc, CHUNK, h, d)
    kp = jnp.pad(kc, ((0, 0), (n_prev, 0), (0, 0), (0, 0), (0, 0)))
    band = jnp.stack([kp[:, j:j + nc] for j in range(n_prev + 1)], axis=2)
    return band.reshape(b, nc, (n_prev + 1) * CHUNK, h, d)

def band_valid(nc, n_prev):
    c = np.arange(nc)[:, None]
    j = np.arange((n_prev + 1) * CHUNK)[None, :]
    return jnp.asarray(c - n_prev + j // CHUNK >= 0)

def band_rel(n_prev):
    i = np.arange(CHUNK)[:, None]
    j = np.arange((n_prev + 1) * CHUNK)[None, :]
    return n_prev * CHUNK + i - j

def chunk_band_attention(q, k, v, n_prev, bias, sinks):
    b, s, hk, g, dh = q.shape
    nc = s // CHUNK
    kw = (n_prev + 1) * CHUNK
    qc = q.reshape(b, nc, CHUNK, hk, g, dh)
    kb = gather_band(k, n_prev)
    vb = gather_band(v, n_prev)
    sc = jnp.einsum('bnqhgd,bnkhd->bnhgqk', qc, kb).astype(jnp.float32) * (dh ** -0.5) + bias
    valid = band_valid(nc, n_prev)[None, :, None, None, None, :]
    sc = jnp.where(valid, sc, NEG_INF)
    if sinks is not None:
        sink = jnp.broadcast_to(sinks.astype(jnp.float32)[None, None, :, :, None, None],
                                sc.shape[:-1] + (1,))
        p = jax.nn.softmax(jnp.concatenate([sc, sink], axis=-1), axis=-1)[..., :kw]
    else:
        p = jax.nn.softmax(sc, axis=-1)
    o = jnp.einsum('bnhgqk,bnkhd->bnqhgd', p.astype(v.dtype), vb)
    return o.reshape(b, s, hk * g * dh)

def alibi_bias():
    slopes = (2.0 ** (-8.0 * np.arange(1, A_Q_HEADS + 1) / A_Q_HEADS)).astype(np.float32)
    dist = np.abs(band_rel(A_PREV_CHUNKS)).astype(np.float32)
    bias = -slopes.reshape(A_KV_HEADS, A_GROUP)[:, :, None, None] * dist[None, None]
    return jnp.asarray(bias)

def rel_pos_bias(table):
    idx = np.clip(band_rel(B_PREV_CHUNKS), -B_REL_CLIP, B_REL_CLIP) + B_REL_CLIP
    return table.astype(jnp.float32)[:, idx][:, None]

def setup_inputs(seed: int = 0) -> dict:
    key = jax.random.key(seed)
    ks = jax.random.split(key, 16)
    f32 = jnp.float32

    def w(k, shape, fan_in):
        return jax.random.normal(k, shape, f32) * (fan_in ** -0.5)

    return {
        "x": jax.random.normal(ks[0], (BATCH, SEQ, D_MODEL), f32),
        "norm_mix_g": 1.0 + 0.05 * jax.random.normal(ks[1], (DEPTH, D_MODEL), f32),
        "w_in": w(ks[2], (DEPTH, D_MODEL, IN_WIDTH), D_MODEL),
        "a_sinks": 0.5 * jax.random.normal(ks[3], (DEPTH, A_KV_HEADS, A_GROUP), f32),
        "b_rel_bias": 0.1 * jax.random.normal(ks[4], (DEPTH, B_HEADS, 2 * B_REL_CLIP + 1), f32),
        "w_branch_a": w(ks[5], (DEPTH, A_WIDTH, D_MODEL), A_WIDTH),
        "w_branch_b": w(ks[6], (DEPTH, B_WIDTH, D_MODEL), B_WIDTH),
        "w_gate": w(ks[7], (DEPTH, D_MODEL, 2 * D_MODEL), D_MODEL),
        "w_out": w(ks[8], (DEPTH, D_MODEL, D_MODEL), D_MODEL),
        "norm_mlp_g": 1.0 + 0.05 * jax.random.normal(ks[9], (DEPTH, D_MODEL), f32),
        "w_mlp_in": w(ks[10], (DEPTH, D_MODEL, D_FF), D_MODEL),
        "w_mlp_out": w(ks[11], (DEPTH, D_FF, D_MODEL), D_FF),
        "norm_final_g": 1.0 + 0.05 * jax.random.normal(ks[12], (D_MODEL,), f32),
    }

def reference(x, norm_mix_g, w_in, a_sinks, b_rel_bias, w_branch_a, w_branch_b, w_gate,
              w_out, norm_mlp_g, w_mlp_in, w_mlp_out, norm_final_g):
    b, s, _ = x.shape
    bias_a = alibi_bias()
    h = x
    for l in range(DEPTH):
        xn = rms_norm(h, norm_mix_g[l])
        proj = xn @ w_in[l]
        o1 = A_WIDTH
        o2 = o1 + A_KV_WIDTH
        o3 = o2 + A_KV_WIDTH
        o4 = o3 + B_WIDTH
        o5 = o4 + B_WIDTH
        q_a = proj[..., :o1].reshape(b, s, A_KV_HEADS, A_GROUP, HEAD_DIM)
        k_a = proj[..., o1:o2].reshape(b, s, A_KV_HEADS, HEAD_DIM)
        v_a = proj[..., o2:o3].reshape(b, s, A_KV_HEADS, HEAD_DIM)
        q_b = proj[..., o3:o4].reshape(b, s, B_HEADS, 1, HEAD_DIM)
        k_b = proj[..., o4:o5].reshape(b, s, B_HEADS, HEAD_DIM)
        v_b = proj[..., o5:].reshape(b, s, B_HEADS, HEAD_DIM)

        att_a = chunk_band_attention(q_a, k_a, v_a, A_PREV_CHUNKS, bias_a, a_sinks[l])
        att_b = chunk_band_attention(q_b, k_b, v_b, B_PREV_CHUNKS,
                                     rel_pos_bias(b_rel_bias[l]), None)

        y_a = att_a @ w_branch_a[l]
        y_b = att_b @ w_branch_b[l]
        gates = jax.nn.sigmoid(xn @ w_gate[l])
        merged = gates[..., :D_MODEL] * y_a + gates[..., D_MODEL:] * y_b
        h = h + merged @ w_out[l]

        hn = rms_norm(h, norm_mlp_g[l])
        u = jnp.square(jax.nn.relu(hn @ w_mlp_in[l]))
        h = h + u @ w_mlp_out[l]
    return rms_norm(h, norm_final_g)


_drawn_inputs = setup_inputs


def setup_inputs(seed=0):
    import zlib

    import numpy as np

    out = dict(_drawn_inputs(seed))
    spreads = {}
    factors = {'norm_mix_g': 4.055, 'a_sinks': 52.776, 'b_rel_bias': 8.0, 'norm_mlp_g': 2.921}
    for name, (base, spread) in spreads.items():
        noise = np.random.default_rng([zlib.crc32(name.encode()), seed]).standard_normal(out[name].shape)
        drawn = base * np.exp(spread * noise) if base else spread * noise
        out[name] = __import__('jax').numpy.asarray(drawn.astype(out[name].dtype))
    for name, factor in factors.items():
        out[name] = (out[name] * factor).astype(out[name].dtype)
    return out
```

```python
from contextlib import ExitStack

import numpy as np

import concourse.bass as bass
from concourse import mybir

F32 = mybir.dt.float32
F32R = mybir.dt.float32r
ALU = mybir.AluOpType
ACT = mybir.ActivationFunctionType
AX = mybir.AxisListType

P = 128
D = 2048
SEQ = 512
CHUNK = 64
DH = 64
A_HEADS, A_KV, B_HEADS = 16, 4, 16
HEADS = A_HEADS + B_HEADS
A_WIDTH, A_KVW, B_WIDTH = A_HEADS * DH, A_KV * DH, B_HEADS * DH
REL = 256
D_FF = 4 * D
EPS = 1e-5
MASKED = -1e30
LOWEST = -3.0e38

KB = D // P
TT = SEQ // P
CB = 256
KU = 4
QC = 512
LAND, SPLIT = 4, 2
FC = D_FF // D
CB_CHUNK = D // CB
STRIP = 512
REL_ROW = 640

BLOCKS = ([("k", "a", 0), ("v", "a", 0), ("q", "a", 0), ("q", "a", 1), ("k", "b", 0), ("q", "a", 2),
           ("v", "b", 0), ("q", "a", 3), ("g", "a", 0), ("g", "b", 0), ("q", "b", 0)]
          + [(kind, "b", g) for g in (1, 2, 3) for kind in "qkv"]
          + [("g", "a", 1), ("g", "b", 1)])
COL0 = {("q", "a"): 0, ("k", "a"): A_WIDTH, ("v", "a"): A_WIDTH + A_KVW,
        ("q", "b"): A_WIDTH + 2 * A_KVW, ("k", "b"): A_WIDTH + 2 * A_KVW + B_WIDTH,
        ("v", "b"): A_WIDTH + 2 * A_KVW + 2 * B_WIDTH}
UNITS1 = KU * len(BLOCKS)

SCORES_AT = [13 + 2 * k for k in range(16)] + [46, 48, 51, 53, 56, 59, 62, 65, 68, 71, 74, 76, 78, 81, 83, 85]
TURN_AT = [n + 1 for n in SCORES_AT]
PV_AT = [n + 2 for n in SCORES_AT]
PV_AT[28] = 81


def block_no(kind, mixer, index):
    return BLOCKS.index((kind, mixer, index))


def ready_count(c):
    return sum(kind != "g" for kind, _, _ in BLOCKS[:c + 1])


def slot_of(mixer, g):
    return 1 if mixer == "a" else g % 2


def head_tiles(h):
    out, at = [], 0
    for t in range(TT):
        first = max(0, t - 1) if h < A_HEADS else 0
        n = (t - first + 1) * P
        if h < A_HEADS:
            bank, col = ((4, 0), (4, P), (5, 0), (5, 2 * P))[t]
        else:
            bank, col = ((4, 0), (4, P), (5, 0), (6, 0))[t]
        out.append((first, n, bank, col, at))
        at += n
    return out


def bank_end(h, t):
    tiles = head_tiles(h)
    return max(i for i in range(TT) if tiles[i][2] == tiles[t][2]) + 1


PV_BANK = 7
PROBS = sum(n for _, n, _, _, _ in head_tiles(HEADS - 1))


def build(nc, x, norm_mix_g, w_in, a_sinks, b_rel_bias, w_branch_a, w_branch_b, w_gate, w_out,
          norm_mlp_g, w_mlp_in, w_mlp_out, norm_final_g, identity_in, alibi_in, out):
    rel_rows = nc.dram_tensor("rel_rows", (B_HEADS, REL_ROW), F32, kind="Internal").ap()

    x_tiles = x[0].rearrange("(t p) d -> p t d", p=P)
    out_tiles = out[0].rearrange("(t p) d -> p t d", p=P)

    def rows(w):
        return w[0].rearrange("(k p) n -> p k n", p=P)

    win, wga, wba, wbb = rows(w_in), rows(w_gate), rows(w_branch_a), rows(w_branch_b)
    wout, wup, wdown = rows(w_out), rows(w_mlp_in), rows(w_mlp_out)

    with ExitStack() as ctx:
        def sb(name, shape, dt=F32, into=ctx):
            return into.enter_context(nc.sbuf_tensor(name, shape, dt))

        def sem(name):
            return ctx.enter_context(nc.semaphore(name))

        bank = ctx.enter_context(nc.psum_tensor("bank", [P, 8, 512], F32))

        landing = sb("landing", [P, LAND, 1024])
        w_hi = sb("w_hi", [P, SPLIT, 1024], F32R)
        w_lo = sb("w_lo", [P, SPLIT, 1024], F32R)
        stream = sb("stream", [P, TT * D])
        xn_hi = sb("xn_hi", [P, KB, SEQ], F32R)
        xn_lo = sb("xn_lo", [P, KB, SEQ], F32R)
        side = sb("side", [P, 4096])
        identity = sb("identity", [P, P])
        sinks = sb("sinks", [P, A_HEADS])
        squares = sb("squares", [P, TT, 4])
        stat = sb("stat", [P, 6, TT])
        neg_max = sb("neg_max", [P, TT])
        row_max = sb("row_max", [P, TT])
        row_sum = sb("row_sum", [P, TT])
        sink_exp = sb("sink_exp", [P, TT])
        row_inv = sb("row_inv", [P, TT])

        first_phase = ExitStack()
        q_hi = sb("q_hi", [P, 4, SEQ], F32R, first_phase)
        q_lo = sb("q_lo", [P, 4, SEQ], F32R, first_phase)
        k_hi = sb("k_hi", [P, 2, 2, SEQ], F32R, first_phase)
        k_lo = sb("k_lo", [P, 2, 2, SEQ], F32R, first_phase)
        v_hi = sb("v_hi", [P, 2, TT, CB], F32R, first_phase)
        v_lo = sb("v_lo", [P, 2, TT, CB], F32R, first_phase)
        pt_hi = sb("pt_hi", [P, TT, 512], F32R, first_phase)
        pt_lo = sb("pt_lo", [P, TT, 512], F32R, first_phase)
        probs = sb("probs", [P, PROBS], F32, first_phase)
        strips = sb("strips", [P, 2, STRIP], F32, first_phase)
        first_phase.close()
        at_hi = sb("at_hi", [P, KB, SEQ], F32R)
        at_lo = sb("at_lo", [P, KB, SEQ], F32R)
        gain_row = sb("gain_row", [P, D])

        x_tok = stream[:].rearrange("p (t d) -> p t d", t=TT)
        feat = stream[:].rearrange("p (k s) -> p k s", k=KB)
        gate = side[:].rearrange("p (s m b n) -> p s m b n", s=2, m=2, b=2)
        x_again = side[:].rearrange("p (s t n) -> p s t n", s=2, t=TT)
        h_norm = side[:].rearrange("p (s d) -> p s d", s=2)
        first_gain = side[:, 0:D]
        rel_table = side[0:B_HEADS, D:D + REL_ROW]
        relu_z = side[:, 0:1024]
        relu_sq = side[:, 1024:2048]

        x_landed = [sem(f"x_landed{t}") for t in range(TT)]
        const_landed = sem("const_landed")
        gain1_landed = sem("gain1_landed")
        rel_landed = sem("rel_landed")
        rel_extended = sem("rel_extended")
        rel_stored = sem("rel_stored")
        squared = sem("squared")
        stat_step = sem("stat_step")
        var_ready = sem("var_ready")
        root_ready = sem("root_ready")
        rms_ready = sem("rms_ready")
        normed = sem("normed")
        turned = sem("turned")
        turned_hi = sem("turned_hi")
        turned_lo = sem("turned_lo")
        unit_landed = [sem(f"unit_landed{s}") for s in range(LAND)]
        unit_hi = sem("unit_hi")
        unit_lo = sem("unit_lo")
        unit_used = sem("unit_used")
        proj_hi = sem("proj_hi")
        proj_ready = sem("proj_ready")
        gate_ready = sem("gate_ready")
        strip_landed = [sem("strip_landed0"), sem("strip_landed1")]
        strip_masked = sem("strip_masked")
        scores_done = sem("scores_done")
        biased = sem("biased")
        max_ready = sem("max_ready")
        exp_done = sem("exp_done")
        sum_step = sem("sum_step")
        probs_ready = sem("probs_ready")
        pt_done = sem("pt_done")
        pt_hi_done = sem("pt_hi_done")
        pt_lo_done = sem("pt_lo_done")
        pv_done = sem("pv_done")
        att_ready = sem("att_ready")
        at_hi_done = sem("at_hi_done")
        at_lo_done = sem("at_lo_done")
        branch_a = sem("branch_a")
        branch_b = sem("branch_b")
        merged = sem("merged")
        merged_hi = sem("merged_hi")
        merged_lo = sem("merged_lo")
        x2_landed = [sem("x2_landed0"), sem("x2_landed1")]
        gain2_landed = sem("gain2_landed")
        gain3_landed = sem("gain3_landed")
        tile_done = sem("tile_done")
        tile_added = sem("tile_added")
        relu_done = sem("relu_done")
        sq_done = sem("sq_done")
        hidden_hi = sem("hidden_hi")
        hidden_lo = sem("hidden_lo")
        final_ready = sem("final_ready")
        stored = sem("stored")

        B2 = UNITS1 // 4
        LOOP2, PER2 = 3, 6
        B2_END = B2 + LOOP2 * PER2
        B3 = B2_END + 2
        B4 = B3 + 8
        N_BLOCKS1 = len(BLOCKS)
        NBR = D // CB

        def quad_of(phase3, q):
            return 4 * ((q + 1) % 2) if phase3 else 4 * (q % 2)

        block = ctx.enter_context(nc.Block())

        @block.sync
        def _(sp):
            def load(b, u, src, width):
                s = u % LAND
                if not (isinstance(b, int) and b == 0):
                    sp.wait_ge(unit_lo, 4 * b + (u - LAND + 1))
                dst = landing[:, s, :].rearrange("p (k n) -> p k n", n=width)
                sp.dma_start(dst, src).then_inc(unit_landed[s], 16)

            def load_block(b, w, col, units=4):
                for u in range(units):
                    load(b, u, w[:, KU * u:KU * (u + 1), bass.ds(col, CB)], CB)

            def strip(h):
                if h >= 2:
                    sp.wait_ge(biased, TT * (h - 1))
                if h < A_HEADS:
                    sp.dma_start(strips[:, h % 2, 0:2 * P], alibi_in[h]).then_inc(strip_landed[h % 2], 16)
                else:
                    if h == A_HEADS:
                        sp.wait_ge(rel_stored, 16)
                    row = bass.AP(rel_rows.tensor, (h - A_HEADS) * REL_ROW, [[1, P], [1, STRIP]])
                    sp.dma_start(strips[:, h % 2, :], row).then_inc(strip_landed[h % 2], 16)

            for t in range(TT):
                sp.dma_start(x_tok[:, t, :], x_tiles[:, t, :]).then_inc(x_landed[t], 16)
                if t == 0:
                    sp.dma_start(first_gain, norm_mix_g[0:1, :].partition_broadcast(P)).then_inc(gain1_landed, 16)
            n = 0
            for c, (kind, mixer, i) in enumerate(BLOCKS):
                if kind == "g":
                    w, col = wga, (0 if mixer == "a" else D) + i * CB
                else:
                    w, col = win, COL0[kind, mixer] + i * CB
                for u in range(KU):
                    load(c, u, w[:, KU * u:KU * (u + 1), col:col + CB], CB)
                    if c == 0 and u == 0:
                        sp.wait_ge(rel_extended, 1)
                        sp.dma_start(rel_rows, rel_table).then_inc(rel_stored, 16)
                        strip(0)
                        strip(1)
                    if n - 6 in SCORES_AT and SCORES_AT.index(n - 6) + 2 < HEADS:
                        strip(SCORES_AT.index(n - 6) + 2)
                    n += 1

            def load_branches(b, nb):
                for u in range(2):
                    load(b, u, wba[:, KU * u:KU * (u + 1), bass.ds(nb * CB, CB)], CB)
                for u in range(2):
                    load(b, 2 + u, wbb[:, KU * u:KU * (u + 1), bass.ds(nb * CB, CB)], CB)

            with sp.Fori(0, LOOP2) as i:
                for j in range(2):
                    b = i * PER2 + (B2 + 3 * j)
                    load_branches(b, i * 2 + j)
                    load_block(b + 1, wga, i * (2 * CB) + (2 + j) * CB)
                    load_block(b + 2, wga, i * (2 * CB) + (D + (2 + j) * CB))
            for j in range(2):
                load_branches(B2_END + j, NBR - 2 + j)

            for q in range(4):
                for u in range(8):
                    load(B3 + 2 * q + u // 4, u % 4, wout[:, 2 * u:2 * u + 2, q * QC:(q + 1) * QC], QC)
                    if u == 5:
                        for r in ((0, 1) if q == 0 else (q + 1,) if q < 3 else ()):
                            if r < 2:
                                sp.wait_ge(merged, NBR)
                            else:
                                sp.wait_ge(tile_added, TT * (r - 1))
                            sp.dma_start(x_again[:, r % 2], x_tiles[:, :, r * QC:(r + 1) * QC])\
                                .then_inc(x2_landed[r % 2], 16)
                    if q == 0 and u == 6:
                        sp.dma_start(gain_row[:], norm_mlp_g[0:1, :].partition_broadcast(P))\
                            .then_inc(gain2_landed, 16)

            def load_up(b, col):
                for j in range(CB_CHUNK):
                    load_block(b + j, wup, col + j * CB)

            def load_down(b, k):
                for q in range(4):
                    for u in range(8):
                        load(b + 2 * q + u // 4, u % 4,
                             wdown[:, bass.ds(k + 2 * u, 2), q * QC:(q + 1) * QC], QC)

            load_up(B4, 0)
            sp.wait_ge(normed, 2 * TT)
            sp.dma_start(gain_row[:], norm_final_g.rearrange("(o d) -> o d", o=1).partition_broadcast(P))\
                .then_inc(gain3_landed, 16)
            with sp.Fori(0, FC - 1) as f:
                load_down(f * 16 + (B4 + 8), f * KB)
                load_up(f * 16 + (B4 + 16), f * D + D)
            load_down(B4 + 16 * (FC - 1) + 8, KB * (FC - 1))
            for t in range(TT):
                sp.wait_ge(final_ready, t + 1)
                sp.dma_start(out_tiles[:, t, :], x_tok[:, t, :]).then_inc(stored, 16)
            sp.wait_ge(stored, 16 * TT)

        @block.scalar
        def _(act):
            def split(b, u):
                s = u % SPLIT
                act.wait_ge(unit_landed[u % LAND], 16 * b + 16)
                if not (isinstance(b, int) and 4 * b + u < SPLIT):
                    act.wait_ge(unit_used, 4 * b + (u - SPLIT + 1))
                nc.scalar.activation(w_hi[:, s, :], landing[:, u % LAND, :], ACT.Copy).then_inc(unit_hi, 1)

            def turn_hi(t, first, x_hi, x_lo):
                for g in range(4):
                    act.wait_ge(turned, first + 4 * t + g + 1)
                    src = bank[:, 4 * (t % 2) + g, :].rearrange("p (k s) -> p k s", k=4)
                    nc.scalar.activation(x_hi[:, 4 * g:4 * g + 4, t * P:(t + 1) * P], src, ACT.Copy)\
                        .then_inc(turned_hi, 1)

            def evacuate(c):
                kind, mixer, i = BLOCKS[c]
                act.wait_ge(unit_used, KU * (c + 1))
                pair = bank[:, 2 * (c % 2):2 * (c % 2) + 2, :]
                if kind == "g":
                    if i == 1:
                        act.wait_ge(rel_stored, 16)
                    nc.scalar.activation(gate[:, i, "ab".index(mixer)], pair, ACT.Sigmoid)\
                        .then_inc(gate_ready, 1)
                    return
                if kind == "q":
                    used = last_scores_before_q(mixer, i)
                    if used:
                        act.wait_ge(scores_done, used)
                    if mixer == "a":
                        r = (i % 2) * DH
                        for hh in range(4):
                            src = bank[(hh % 2) * DH:(hh % 2 + 1) * DH, 2 * (c % 2) + hh // 2, :]
                            ins = nc.scalar.activation(q_hi[r:r + DH, hh, :], src, ACT.Copy, scale=DH ** -0.5)
                    else:
                        ins = nc.scalar.activation(q_hi[:, 2 * (i % 2):2 * (i % 2) + 2, :], pair, ACT.Copy,
                                                   scale=DH ** -0.5)
                elif kind == "k":
                    if mixer == "b" and i:
                        act.wait_ge(scores_done, A_HEADS + 4 * (i - 1))
                    ins = nc.scalar.activation(k_hi[:, slot_of(mixer, i)], pair, ACT.Copy)
                else:
                    if mixer == "b" and i:
                        act.wait_ge(pv_done, A_HEADS + 4 * (i - 1))
                    ins = nc.scalar.activation(v_hi[:, slot_of(mixer, i)].rearrange("p t n -> p (t n)"),
                                               pair.rearrange("p b n -> p (b n)"), ACT.Copy)
                ins.then_inc(proj_hi, 1)

            def exponentials(h):
                act.wait_ge(max_ready, h + 1)
                if h < A_HEADS:
                    nc.scalar.activation(sink_exp[:], neg_max[:], ACT.Exp, bias=sinks[:, h:h + 1])
                for t, (_, n, _, _, at) in enumerate(head_tiles(h)):
                    nc.scalar.activation(probs[:, at:at + n], probs[:, at:at + n], ACT.Exp,
                                         bias=neg_max[:, t:t + 1], accum_out=row_sum[:, t:t + 1])\
                        .then_inc(exp_done, 1)

            def turned_probs(h):
                for t, (first, n, bk, col, _) in enumerate(head_tiles(h)):
                    act.wait_ge(pt_done, TT * h + bank_end(h, t))
                    nc.scalar.activation(pt_hi[:, t, first * P:first * P + n], bank[:, bk, col:col + n], ACT.Copy)\
                        .then_inc(pt_hi_done, 1)

            def attended(h):
                act.wait_ge(pv_done, h + 1)
                r = (h // 4 % 2 if h < A_HEADS else h % 2) * DH
                o = (h % 2) * DH
                nc.scalar.activation(feat[o:o + DH, h // 2, :], bank[r:r + DH, PV_BANK, :], ACT.Copy)\
                    .then_inc(att_ready, 1)

            def stage(n):
                if n >= 0 and n % KU == KU - 1 and n // KU < N_BLOCKS1:
                    evacuate(n // KU)
                if n in PV_AT:
                    attended(PV_AT.index(n))
                if n in SCORES_AT:
                    exponentials(SCORES_AT.index(n))
                if n in TURN_AT:
                    turned_probs(TURN_AT.index(n))

            act.dma_start(rel_table[:, 0:REL + P], b_rel_bias[0, :, REL - P + 1:2 * REL + 1]).then_inc(rel_landed, 16)
            act.dma_start(identity[:], identity_in).then_inc(const_landed, 16)
            act.dma_start(sinks[:], a_sinks.rearrange("o k g -> o (k g)").partition_broadcast(P))\
                .then_inc(const_landed, 16)

            def mean_square(t):
                act.wait_ge(x_landed[t], 16)
                nc.scalar.activation(pt_hi[:].rearrange("p t s -> p (t s)"), x_tok[:, t, :], ACT.Square,
                                     accum_out=squares[:, t, 0:1]).then_inc(squared, 1)

            def root(t):
                act.wait_ge(var_ready, t + 1)
                nc.scalar.activation(stat[:, 2, t:t + 1], stat[:, 1, t:t + 1], ACT.Sqrt).then_inc(root_ready, 1)

            for t in range(TT):
                mean_square(t)
                root(t)
                if t == TT - 1:
                    split(0, 0)
                if t >= 1:
                    turn_hi(t - 1, 0, xn_hi, xn_lo)
            turn_hi(TT - 1, 0, xn_hi, xn_lo)

            for n in range(1, UNITS1):
                split(n // 4, n % 4)
                stage(n - 2)
            split(B2, 0)
            stage(UNITS1 - 2)
            split(B2, 1)
            attended(HEADS - 1)
            for g in range(KB // 2):
                if g == KB // 2 - 1:
                    act.wait_ge(att_ready, HEADS)
                nc.scalar.activation(at_hi[:, 2 * g:2 * g + 2, :], feat[:, 2 * g:2 * g + 2, :], ACT.Copy)\
                    .then_inc(at_hi_done, 1)
            evacuate(N_BLOCKS1 - 1)

            def gates(b, u, s, m, nb):
                act.wait_ge(unit_used, 4 * b + (u + 1))
                act.wait_ge(merged, nb - 1)
                nc.scalar.activation(gate[:, s, m], bank[:, 2 * m:2 * m + 2, :], ACT.Sigmoid)\
                    .then_inc(gate_ready, 1)

            with act.Fori(0, LOOP2) as i:
                for j in range(2):
                    b = i * PER2 + (B2 + 3 * j)
                    nb = i * 2 + j
                    if j == 1:
                        split(b, 0)
                        split(b, 1)
                        gates(b - 1, 3, 0, 1, nb + 1)
                    split(b, 2)
                    split(b, 3)
                    for u in range(4):
                        split(b + 1, u)
                    split(b + 2, 0)
                    split(b + 2, 1)
                    gates(b + 1, 3, j, 0, nb + 2)
                    split(b + 2, 2)
                    split(b + 2, 3)
                split(i * PER2 + (B2 + PER2), 0)
                split(i * PER2 + (B2 + PER2), 1)
                gates(i * PER2 + (B2 + PER2 - 1), 3, 1, 1, i * 2 + 3)

            def merged_part(nb):
                act.wait_ge(merged, nb + 1)
                nc.scalar.activation(xn_hi[:, 2 * nb:2 * nb + 2, :], feat[:, 2 * nb:2 * nb + 2, :], ACT.Copy)\
                    .then_inc(merged_hi, 1)

            merged_part(0)
            split(B2_END, 2)
            merged_part(1)
            split(B2_END, 3)
            merged_part(2)
            for u in range(4):
                split(B2_END + 1, u)
                merged_part(3 + u)

            def sum_squares(q, t):
                nc.scalar.activation(at_hi[:, TT * q + t, :], x_tok[:, t, q * QC:(q + 1) * QC], ACT.Square,
                                     accum_out=squares[:, t, q:q + 1]).then_inc(squared, 1)

            def out_quarter(b, first_tile, prev, extra=None):
                for u in range(8):
                    split(b + u // 4, u % 4)
                    if u == 1 and extra is not None:
                        extra()
                    if u == 2 and prev is not None:
                        for t in range(TT):
                            act.wait_ge(tile_added, first_tile + t + 1)
                            sum_squares(prev, t)

            out_quarter(B3, 0, None, lambda: merged_part(NBR - 1))
            for q in range(1, 4):
                out_quarter(B3 + 2 * q, TT * (q - 1), q - 1)
            split(B4, 0)
            split(B4, 1)
            for t in range(TT):
                act.wait_ge(tile_added, 3 * TT + t + 1)
                sum_squares(3, t)
            act.wait_ge(var_ready, TT + 1)
            nc.scalar.activation(stat[:, 2, :], stat[:, 1, :], ACT.Sqrt).then_inc(root_ready, 1)
            for t in range(TT):
                turn_hi(t, 4 * TT, at_hi, at_lo)

            def hidden(b, j, count):
                act.wait_ge(unit_used, 4 * b + 4)
                nc.scalar.activation(relu_z, bank[:, 2 * (j % 4):2 * (j % 4) + 2, :].rearrange("p b n -> p (b n)"),
                                     ACT.Relu).then_inc(relu_done, 1)
                act.wait_ge(sq_done, count + 1)
                nc.scalar.activation(xn_hi[:, 2 * j:2 * j + 2, :].rearrange("p b n -> p (b n)"), relu_sq, ACT.Copy)\
                    .then_inc(hidden_hi, 1)

            def up(b, count, started):
                for j in range(CB_CHUNK):
                    for u in range(4):
                        if j or u > 1 or not started:
                            split(b + j, u)
                        if u == 1 and j:
                            hidden(b + j - 1, j - 1, count + (j - 1))

            def down(b, count):
                for q in range(4):
                    for u in range(8):
                        split(b + 2 * q + u // 4, u % 4)
                        if q == 0 and u == 1:
                            hidden(b - 1, CB_CHUNK - 1, count + (CB_CHUNK - 1))

            up(B4, 0, True)
            with act.Fori(0, FC - 1) as f:
                down(f * 16 + (B4 + 8), f * CB_CHUNK)
                up(f * 16 + (B4 + 16), f * CB_CHUNK + CB_CHUNK, False)
            last = B4 + 16 * (FC - 1) + 8
            tiles_before = 4 * TT + 4 * TT * (FC - 1)
            for q in range(4):
                for u in range(8):
                    split(last + 2 * q + u // 4, u % 4)
                    if q == 0 and u == 1:
                        hidden(last - 1, CB_CHUNK - 1, CB_CHUNK * FC - 1)
                    if q > 0 and u == 2:
                        for t in range(TT):
                            act.wait_ge(tile_added, tiles_before + TT * (q - 1) + t + 1)
                            sum_squares(q - 1, t)
            for t in range(TT):
                act.wait_ge(tile_added, tiles_before + 3 * TT + t + 1)
                sum_squares(3, t)
            act.wait_ge(var_ready, TT + 2)
            nc.scalar.activation(stat[:, 2, :], stat[:, 1, :], ACT.Sqrt).then_inc(root_ready, 1)

        @block.vector
        def _(dve):
            steps = [0]

            def step(ins):
                steps[0] += 1
                ins.then_inc(stat_step, 1)
                dve.wait_ge(stat_step, steps[0])

            def split(b, u):
                s = u % SPLIT
                dve.wait_ge(unit_hi, 4 * b + (u + 1))
                nc.vector.tensor_tensor(w_lo[:, s, :], landing[:, u % LAND, :], w_hi[:, s, :].bitcast(F32),
                                        ALU.subtract).then_inc(unit_lo, 1)

            def inverse_rms(t0, t1, quarters, squares_count, roots_count):
                dve.wait_ge(squared, squares_count)
                if quarters > 1:
                    step(nc.vector.tensor_reduce(stat[:, 0, t0:t1], squares[:, t0:t1, 0:quarters], AX.X, ALU.add))
                    total = stat[:, 0, t0:t1]
                else:
                    total = squares[:, t0:t1, 0:1].rearrange("p t o -> p (t o)")
                v, root, r, a, c = (stat[:, k, t0:t1] for k in (1, 2, 3, 4, 5))
                nc.vector.tensor_scalar(v, total, 1.0 / D, EPS, ALU.mult, ALU.add).then_inc(var_ready, 1)
                dve.wait_ge(root_ready, roots_count)
                step(nc.vector.reciprocal(r, root))
                step(nc.vector.tensor_tensor(a, r, r, ALU.mult))
                step(nc.vector.tensor_tensor(c, a, v, ALU.mult))
                step(nc.vector.tensor_scalar(a, c, -0.5, 1.5, ALU.mult, ALU.add))
                step(nc.vector.tensor_tensor(c, r, a, ALU.mult))
                return c

            def turn_lo(t, first, x_hi, x_lo):
                for g in range(4):
                    dve.wait_ge(turned_hi, first + 4 * t + g + 1)
                    src = bank[:, 4 * (t % 2) + g, :].rearrange("p (k s) -> p k s", k=4)
                    nc.vector.tensor_tensor(x_lo[:, 4 * g:4 * g + 4, t * P:(t + 1) * P], src,
                                            x_hi[:, 4 * g:4 * g + 4, t * P:(t + 1) * P].bitcast(F32),
                                            ALU.subtract).then_inc(turned_lo, 1)

            def evacuate(c):
                kind, mixer, i = BLOCKS[c]
                if kind == "g":
                    return
                dve.wait_ge(proj_hi, ready_count(c))
                pair = bank[:, 2 * (c % 2):2 * (c % 2) + 2, :]
                if kind == "q":
                    if mixer == "a":
                        r = (i % 2) * DH
                        for hh in range(4):
                            src = bank[(hh % 2) * DH:(hh % 2 + 1) * DH, 2 * (c % 2) + hh // 2, :]
                            ins = nc.vector.scalar_tensor_tensor(
                                out=q_lo[r:r + DH, hh, :], in0=src, scalar=DH ** -0.5,
                                in1=q_hi[r:r + DH, hh, :].bitcast(F32), op0=ALU.mult, op1=ALU.subtract)
                    else:
                        s = slice(2 * (i % 2), 2 * (i % 2) + 2)
                        ins = nc.vector.scalar_tensor_tensor(
                            out=q_lo[:, s, :], in0=pair, scalar=DH ** -0.5, in1=q_hi[:, s, :].bitcast(F32),
                            op0=ALU.mult, op1=ALU.subtract)
                else:
                    s = slot_of(mixer, i)
                    if kind == "k":
                        hi, lo = k_hi[:, s], k_lo[:, s]
                    else:
                        hi, lo = (y[:, s].rearrange("p t n -> p (t n)") for y in (v_hi, v_lo))
                        pair = pair.rearrange("p b n -> p (b n)")
                    ins = nc.vector.tensor_tensor(lo, pair, hi.bitcast(F32), ALU.subtract)
                ins.then_inc(proj_ready, 1)

            def biased_scores(h):
                s = h % 2
                dve.wait_ge(strip_landed[s], 16 * (h // 2 + 1))
                if h >= A_HEADS:
                    nc.vector.memset(strips[0:CHUNK, s, 0:CHUNK], MASKED).then_inc(strip_masked, 1)
                    dve.wait_ge(strip_masked, h - A_HEADS + 1)
                dve.wait_ge(scores_done, h + 1)
                if h:
                    dve.wait_ge(pt_done, TT * h)
                for t, (_, n, bk, col, at) in enumerate(head_tiles(h)):
                    part = strips[:, s, 0:n]
                    reverse = bass.AP(part.tensor, part.offset + n - 1, [part.ap[0], [-1, n]])
                    nc.vector.tensor_tensor_reduce(
                        out=probs[:, at:at + n], in0=bank[:, bk, col:col + n], in1=reverse, scale=1.0,
                        scalar=LOWEST, op0=ALU.add, op1=ALU.max, accum_out=row_max[:, t:t + 1]).then_inc(biased, 1)
                dve.wait_ge(biased, TT * (h + 1))
                if h < A_HEADS:
                    nc.vector.tensor_scalar(neg_max[:], row_max[:], sinks[:, h:h + 1], -1.0, ALU.max,
                                            ALU.mult).then_inc(max_ready, 1)
                else:
                    nc.vector.tensor_scalar(neg_max[:], row_max[:], -1.0, None, ALU.mult).then_inc(max_ready, 1)

            sum_steps = [0]

            def normalise(h):
                dve.wait_ge(exp_done, TT * (h + 1))
                if h < A_HEADS:
                    sum_steps[0] += 1
                    nc.vector.tensor_tensor(row_max[:], row_sum[:], sink_exp[:], ALU.add).then_inc(sum_step, 1)
                    dve.wait_ge(sum_step, sum_steps[0])
                sum_steps[0] += 1
                nc.vector.reciprocal(row_inv[:], row_max[:] if h < A_HEADS else row_sum[:]).then_inc(sum_step, 1)
                dve.wait_ge(sum_step, sum_steps[0])
                for t, (_, n, _, _, at) in enumerate(head_tiles(h)):
                    nc.vector.tensor_scalar(probs[:, at:at + n], probs[:, at:at + n], row_inv[:, t:t + 1], None,
                                            ALU.mult).then_inc(probs_ready, 1)

            def turned_probs(h):
                for t, (first, n, bk, col, _) in enumerate(head_tiles(h)):
                    dve.wait_ge(pt_hi_done, TT * h + bank_end(h, t))
                    nc.vector.tensor_tensor(pt_lo[:, t, first * P:first * P + n], bank[:, bk, col:col + n],
                                            pt_hi[:, t, first * P:first * P + n].bitcast(F32), ALU.subtract)\
                        .then_inc(pt_lo_done, 1)

            dve.wait_ge(rel_landed, 16)
            last = REL + P
            nc.vector.tensor_copy(rel_table[:, last:REL_ROW],
                                  rel_table[:, last - 1:last].broadcast_to([B_HEADS, REL_ROW - last]))\
                .then_inc(rel_extended, 1)

            def normalise_first(t):
                c = inverse_rms(t, t + 1, 1, t + 1, t + 1)
                if t == 0:
                    dve.wait_ge(gain1_landed, 16)
                nc.vector.scalar_tensor_tensor(out=x_tok[:, t, :], in0=x_tok[:, t, :], scalar=c, in1=first_gain,
                                               op0=ALU.mult, op1=ALU.mult).then_inc(normed, 1)

            for t in range(TT):
                normalise_first(t)
                if t == TT - 1:
                    split(0, 0)
                if t >= 1:
                    turn_lo(t - 1, 0, xn_hi, xn_lo)
            turn_lo(TT - 1, 0, xn_hi, xn_lo)

            for n in range(1, UNITS1 + 1):
                m = n - 2
                head = SCORES_AT.index(m) if m in SCORES_AT else None
                if head is not None:
                    biased_scores(head)
                split(n // 4, n % 4)
                if m in TURN_AT:
                    turned_probs(TURN_AT.index(m))
                if m >= 0 and m % KU == KU - 1:
                    evacuate(m // KU)
                if head is not None:
                    normalise(head)
            split(B2, 1)
            for g in range(KB // 2):
                dve.wait_ge(at_hi_done, g + 1)
                nc.vector.tensor_tensor(at_lo[:, 2 * g:2 * g + 2, :], feat[:, 2 * g:2 * g + 2, :],
                                        at_hi[:, 2 * g:2 * g + 2, :].bitcast(F32), ALU.subtract)\
                    .then_inc(at_lo_done, 1)

            def scaled_a(b, s, nb):
                dve.wait_ge(unit_used, 4 * b + 2)
                dve.wait_ge(gate_ready, 2 * nb + 2)
                nc.vector.tensor_tensor(feat[:, bass.ds(2 * nb, 2), :], gate[:, s, 0], bank[:, 0:2, :], ALU.mult)\
                    .then_inc(branch_a, 1)

            def merge_b(b, s, nb):
                dve.wait_ge(unit_used, 4 * b + 4)
                nc.vector.tensor_tensor(gate[:, s, 1], gate[:, s, 1], bank[:, 2:4, :], ALU.mult)\
                    .then_inc(branch_b, 1)
                dve.wait_ge(branch_a, nb + 1)
                dve.wait_ge(branch_b, nb + 1)
                nc.vector.tensor_tensor(feat[:, bass.ds(2 * nb, 2), :], feat[:, bass.ds(2 * nb, 2), :],
                                        gate[:, s, 1], ALU.add).then_inc(merged, 1)

            with dve.Fori(0, LOOP2) as i:
                for j in range(2):
                    b = i * PER2 + (B2 + 3 * j)
                    nb = i * 2 + j
                    if j == 1:
                        split(b, 0)
                        split(b, 1)
                    split(b, 2)
                    split(b, 3)
                    scaled_a(b, j, nb)
                    split(b + 1, 0)
                    split(b + 1, 1)
                    merge_b(b, j, nb)
                    split(b + 1, 2)
                    split(b + 1, 3)
                    for u in range(4):
                        split(b + 2, u)
                split(i * PER2 + (B2 + PER2), 0)
                split(i * PER2 + (B2 + PER2), 1)

            def merged_part(nb):
                dve.wait_ge(merged_hi, nb + 1)
                nc.vector.tensor_tensor(xn_lo[:, 2 * nb:2 * nb + 2, :], feat[:, 2 * nb:2 * nb + 2, :],
                                        xn_hi[:, 2 * nb:2 * nb + 2, :].bitcast(F32), ALU.subtract)\
                    .then_inc(merged_lo, 1)

            merged_part(0)
            split(B2_END, 2)
            merged_part(1)
            split(B2_END, 3)
            scaled_a(B2_END, 0, NBR - 2)
            merged_part(2)
            for u in range(4):
                split(B2_END + 1, u)
                if u == 1:
                    merge_b(B2_END, 0, NBR - 2)
                if u == 3:
                    scaled_a(B2_END + 1, 1, NBR - 1)
                merged_part(3 + u)

            def tile_complete(t, quarter, b):
                if t < TT - 1:
                    dve.wait_ge(tile_done, (TT - 1) * quarter + (t + 1))
                else:
                    dve.wait_ge(unit_used, 4 * b + 8)

            def residual(q, t, quarter, b):
                tile_complete(t, quarter, b)
                dst = x_tok[:, t, q * QC:(q + 1) * QC]
                nc.vector.tensor_tensor(dst, dst, bank[:, quad_of(False, q) + t, :], ALU.add)\
                    .then_inc(tile_added, 1)

            def residual3(q):
                dve.wait_ge(x2_landed[q % 2], 16 * (q // 2 + 1))
                for t in range(TT):
                    tile_complete(t, q, B3 + 2 * q)
                    nc.vector.tensor_tensor(x_tok[:, t, q * QC:(q + 1) * QC], x_again[:, q % 2, t, :],
                                            bank[:, quad_of(True, q) + t, :], ALU.add).then_inc(tile_added, 1)

            for q in range(4):
                for u in range(8):
                    split(B3 + 2 * q + u // 4, u % 4)
                    if q == 0 and u == 1:
                        merge_b(B2_END + 1, 1, NBR - 1)
                        merged_part(NBR - 1)
                    if q > 0 and u == 1:
                        residual3(q - 1)
            split(B4, 0)
            split(B4, 1)
            residual3(3)
            c = inverse_rms(0, TT, 4, TT + 4 * TT, TT + 1)
            dve.wait_ge(gain2_landed, 16)
            for t in range(TT):
                if t >= 2:
                    dve.wait_ge(turned, 4 * TT + 4 * (t - 1))
                nc.vector.scalar_tensor_tensor(out=h_norm[:, t % 2, :], in0=x_tok[:, t, :], scalar=c[:, t:t + 1],
                                               in1=gain_row[:], op0=ALU.mult, op1=ALU.mult).then_inc(normed, 1)
                if t >= 1:
                    turn_lo(t - 1, 4 * TT, at_hi, at_lo)
            turn_lo(TT - 1, 4 * TT, at_hi, at_lo)

            def hidden(j, count):
                dve.wait_ge(relu_done, count + 1)
                nc.vector.scalar_tensor_tensor(
                    out=relu_sq, in0=bank[:, 2 * (j % 4):2 * (j % 4) + 2, :].rearrange("p b n -> p (b n)"),
                    scalar=0.0, in1=relu_z, op0=ALU.max, op1=ALU.mult).then_inc(sq_done, 1)
                dve.wait_ge(hidden_hi, count + 1)
                nc.vector.tensor_tensor(xn_lo[:, 2 * j:2 * j + 2, :].rearrange("p b n -> p (b n)"), relu_sq,
                                        xn_hi[:, 2 * j:2 * j + 2, :].rearrange("p b n -> p (b n)").bitcast(F32),
                                        ALU.subtract).then_inc(hidden_lo, 1)

            def up(b, count, started, quarter):
                for j in range(CB_CHUNK):
                    for u in range(4):
                        if j or u > 1 or not started:
                            split(b + j, u)
                        if u == 1 and j:
                            hidden(j - 1, count + (j - 1))
                        if u == 1 and not j and quarter is not None:
                            for t in range(TT):
                                residual(3, t, quarter + 3, b - 2)

            def down(b, count, quarter):
                for q in range(4):
                    for u in range(8):
                        split(b + 2 * q + u // 4, u % 4)
                        if q == 0 and u == 1:
                            hidden(CB_CHUNK - 1, count + (CB_CHUNK - 1))
                        if q > 0 and u == 1:
                            for t in range(TT):
                                residual(q - 1, t, quarter + (q - 1), b + 2 * (q - 1))

            up(B4, 0, True, None)
            with dve.Fori(0, FC - 1) as f:
                down(f * 16 + (B4 + 8), f * CB_CHUNK, f * 4 + 4)
                up(f * 16 + (B4 + 16), f * CB_CHUNK + CB_CHUNK, False, f * 4 + 4)
            last = B4 + 16 * (FC - 1) + 8
            down(last, CB_CHUNK * (FC - 1), 4 * FC)
            for t in range(TT):
                residual(3, t, 4 * FC + 3, last + 6)
            c = inverse_rms(0, TT, 4, TT + 8 * TT, TT + 2)
            dve.wait_ge(gain3_landed, 16)
            for t in range(TT):
                nc.vector.scalar_tensor_tensor(out=x_tok[:, t, :], in0=x_tok[:, t, :], scalar=c[:, t:t + 1],
                                               in1=gain_row[:], op0=ALU.mult, op1=ALU.mult)\
                    .then_inc(final_ready, 1)

        @block.tensor
        def _(pe):
            def product(dst, a_hi, a_lo, b_hi, b_lo, start, stop, **kw):
                nc.tensor.matmul(dst, a_hi, b_hi, start=start, stop=False, **kw)
                nc.tensor.matmul(dst, a_hi, b_lo, start=False, stop=False, **kw)
                return nc.tensor.matmul(dst, a_lo, b_hi, start=False, stop=stop, **kw)

            def turn(t, first, src):
                pe.wait_ge(normed, first // 4 + t + 1)
                for g in range(4):
                    if t >= 2 or first:
                        if t >= 2:
                            pe.wait_ge(turned_lo, first + 4 * (t - 2) + g + 1)
                    for k in range(4):
                        ins = nc.tensor.transpose(bank[:, 4 * (t % 2) + g, k * P:(k + 1) * P],
                                                  src[:, (4 * g + k) * P:(4 * g + k + 1) * P], identity[:])
                    ins.then_inc(turned, 1)

            def features(b, u, pair, k0, first, last, x_hi, x_lo):
                pe.wait_ge(unit_lo, 4 * b + (u + 1))
                s = u % SPLIT
                wh = w_hi[:, s, :].rearrange("p (k n) -> p k n", n=CB)
                wl = w_lo[:, s, :].rearrange("p (k n) -> p k n", n=CB)
                for nb in range(2):
                    for k in range(KU):
                        cols = slice(nb * P, (nb + 1) * P)
                        ins = product(bank[:, pair + nb, :], wh[:, k, cols], wl[:, k, cols],
                                      x_hi[:, k0 + k, :], x_lo[:, k0 + k, :],
                                      first and k == 0, last and k == KU - 1)
                ins.then_inc(unit_used, 1)

            def values(b, u, pair):
                pe.wait_ge(unit_lo, 4 * b + (u + 1))
                s = u % SPLIT
                wh = w_hi[:, s, :].rearrange("p (k n) -> p k n", n=CB)
                wl = w_lo[:, s, :].rearrange("p (k n) -> p k n", n=CB)
                for k in range(KU):
                    for t in range(TT):
                        cols = slice(t * P, (t + 1) * P)
                        kb = KU * u + k
                        dst = bank[:, pair + t // 2, (t % 2) * CB:(t % 2 + 1) * CB]
                        ins = product(dst, xn_hi[:, kb, cols], xn_lo[:, kb, cols], wh[:, k, :], wl[:, k, :],
                                      kb == 0 and t % 2 == 0, kb == KB - 1, skip_group_check=True)
                ins.then_inc(unit_used, 1)

            def scores(h):
                mixer, g = ("a", h // 4) if h < A_HEADS else ("b", (h - A_HEADS) // 4)
                hh = h % 4
                if h:
                    pe.wait_ge(pt_lo_done, TT * h)
                pe.wait_ge(proj_ready, max(ready_count(block_no(kind, mixer, g if kind == "q" or mixer == "b" else 0))
                                           for kind in "qk"))
                if mixer == "a":
                    r, qb, kb = (g % 2) * DH, hh, g // 2
                else:
                    r, qb, kb = (hh % 2) * DH, 2 * (g % 2) + hh // 2, hh // 2
                s = slot_of(mixer, g)
                for t, (first, n, bk, col, _) in enumerate(head_tiles(h)):
                    qs, ks = slice(t * P, (t + 1) * P), slice(first * P, first * P + n)
                    ins = product(bank[:, bk, col:col + n], q_hi[r:r + DH, qb, qs], q_lo[r:r + DH, qb, qs],
                                  k_hi[r:r + DH, s, kb, ks], k_lo[r:r + DH, s, kb, ks], True, True)
                ins.then_inc(scores_done, 1)

            def turn_probs(h):
                for t, (_, n, bk, col, at) in enumerate(head_tiles(h)):
                    pe.wait_ge(probs_ready, TT * h + t + 1)
                    for k in range(n // P):
                        ins = nc.tensor.transpose(bank[:, bk, col + k * P:col + (k + 1) * P],
                                                  probs[:, at + k * P:at + (k + 1) * P], identity[:])
                    ins.then_inc(pt_done, 1)

            def times_v(h):
                mixer, g = ("a", 0) if h < A_HEADS else ("b", (h - A_HEADS) // 4)
                pair = (h // 8) if h < A_HEADS else (h % 4) // 2
                s = slot_of(mixer, g)
                pe.wait_ge(proj_ready, ready_count(block_no("v", mixer, g)))
                pe.wait_ge(pt_lo_done, TT * (h + 1))
                if h:
                    pe.wait_ge(att_ready, h)
                for j in range(TT):
                    last = min(j + 2, TT) if h < A_HEADS else TT
                    vh = v_hi[:, s, j, pair * P:(pair + 1) * P]
                    vl = v_lo[:, s, j, pair * P:(pair + 1) * P]
                    ins = product(bank[:, PV_BANK, j * P:last * P].rearrange("p (t q) -> p t q", q=P), vh, vl,
                                  pt_hi[:, j:last, j * P:(j + 1) * P], pt_lo[:, j:last, j * P:(j + 1) * P],
                                  j == 0, j == TT - 1, skip_group_check=True)
                ins.then_inc(pv_done, 1)

            pe.wait_ge(const_landed, 32)
            for t in range(TT):
                turn(t, 0, x_tok[:, t, :])
            pe.wait_ge(turned_lo, 4 * TT)

            for n in range(UNITS1):
                c, u = n // KU, n % KU
                kind, _, _ = BLOCKS[c]
                if u == 0 and c >= 2:
                    if BLOCKS[c - 2][0] == "g":
                        pe.wait_ge(gate_ready, c - 1 - ready_count(c - 2))
                    else:
                        pe.wait_ge(proj_ready, ready_count(c - 2))
                if kind == "v":
                    values(c, u, 2 * (c % 2))
                else:
                    features(c, u, 2 * (c % 2), KU * u, u == 0, u == KU - 1, xn_hi, xn_lo)
                if n in PV_AT:
                    times_v(PV_AT.index(n))
                if n in SCORES_AT:
                    scores(SCORES_AT.index(n))
                if n in TURN_AT:
                    turn_probs(TURN_AT.index(n))

            def branches(b, nb):
                pe.wait_ge(gate_ready, 2 * nb + 3)
                for u in range(2):
                    features(b, u, 0, KU * u, u == 0, u == 1, at_hi, at_lo)
                pe.wait_ge(gate_ready, 2 * nb + 4)
                for u in range(2):
                    features(b, 2 + u, 2, KB // 2 + KU * u, u == 0, u == 1, at_hi, at_lo)

            def gate_block(b, pair, left):
                pe.wait_ge(branch_b if pair else branch_a, left)
                for u in range(4):
                    features(b, u, 2 * pair, KU * u, u == 0, u == 3, xn_hi, xn_lo)

            pe.wait_ge(at_lo_done, KB // 2)
            with pe.Fori(0, LOOP2) as i:
                for j in range(2):
                    b = i * PER2 + (B2 + 3 * j)
                    nb = i * 2 + j
                    branches(b, nb)
                    gate_block(b + 1, 0, nb + 1)
                    gate_block(b + 2, 1, nb + 1)
            branches(B2_END, NBR - 2)
            pe.wait_ge(branch_a, NBR - 1)
            for u in range(2):
                features(B2_END + 1, u, 0, KU * u, u == 0, u == 1, at_hi, at_lo)
            pe.wait_ge(branch_b, NBR - 1)
            for u in range(2):
                features(B2_END + 1, 2 + u, 2, KB // 2 + KU * u, u == 0, u == 1, at_hi, at_lo)

            def quarter(b, first_bank, before, x_hi, x_lo, ready=None):
                for u in range(8):
                    pe.wait_ge(unit_lo, 4 * b + (u + 1))
                    s = u % SPLIT
                    wh = w_hi[:, s, :].rearrange("p (k n) -> p k n", n=QC)
                    wl = w_lo[:, s, :].rearrange("p (k n) -> p k n", n=QC)
                    if ready is not None:
                        ready(u)
                    for k in range(2):
                        kb = 2 * u + k
                        for t in range(TT):
                            if kb == 0:
                                before(t)
                            cols = slice(t * P, (t + 1) * P)
                            ins = product(bank[:, first_bank + t, :], x_hi[:, kb, cols], x_lo[:, kb, cols],
                                          wh[:, k, :], wl[:, k, :], kb == 0, kb == KB - 1)
                            if kb == KB - 1 and t < TT - 1:
                                ins.then_inc(tile_done, 1)
                    ins.then_inc(unit_used, 1)

            def before3(q):
                def wait(t):
                    if q == 0 and t == 0:
                        pe.wait_ge(att_ready, HEADS)
                    if q == 1 and t == 0:
                        pe.wait_ge(branch_b, NBR)
                    if q >= 2:
                        pe.wait_ge(tile_added, TT * (q - 2) + t + 1)
                return wait

            for q in range(4):
                quarter(B3 + 2 * q, quad_of(True, q), before3(q), xn_hi, xn_lo,
                        (lambda u: pe.wait_ge(merged_lo, u + 1)) if q == 0 else None)

            for t in range(TT):
                if t < 2:
                    pe.wait_ge(tile_added, 4 * TT)
                turn(t, 4 * TT, h_norm[:, t % 2, :])
            pe.wait_ge(turned_lo, 8 * TT)

            def up(b, count, tiles):
                for j in range(CB_CHUNK):
                    if j >= 4:
                        pe.wait_ge(hidden_lo, count + (j - 3))
                    elif tiles is not None:
                        pe.wait_ge(tile_added, tiles + 2 * TT + 2 * j + 2)
                    for u in range(4):
                        features(b + j, u, 2 * (j % 4), KU * u, u == 0, u == 3, at_hi, at_lo)

            def down(b, count, tiles):
                for q in range(4):
                    def before(t, q=q):
                        if q < 2 and t % 2 == 0:
                            pe.wait_ge(hidden_lo, count + (5 + 2 * q + t // 2))
                        if q >= 2:
                            pe.wait_ge(tile_added, tiles + (TT * (q - 2) + t + 1))

                    def ready(u):
                        pe.wait_ge(hidden_lo, count + (u + 1))

                    quarter(b + 2 * q, quad_of(False, q), before, xn_hi, xn_lo, ready if q == 0 else None)

            up(B4, 0, None)
            with pe.Fori(0, FC - 1) as f:
                tiles = f * (4 * TT) + 4 * TT
                down(f * 16 + (B4 + 8), f * CB_CHUNK, tiles)
                up(f * 16 + (B4 + 16), f * CB_CHUNK + CB_CHUNK, tiles)
            down(B4 + 16 * (FC - 1) + 8, CB_CHUNK * (FC - 1), 4 * TT * FC)


def last_scores_before_q(mixer, i):
    if mixer == "a":
        return 4 * (i - 1) if i >= 2 else 0
    return A_HEADS if i == 0 else A_HEADS if i == 1 else A_HEADS + 4 * (i - 1)


_INS = ["x", "norm_mix_g", "w_in", "a_sinks", "b_rel_bias", "w_branch_a", "w_branch_b", "w_gate",
        "w_out", "norm_mlp_g", "w_mlp_in", "w_mlp_out", "norm_final_g"]


def alibi_strips():
    slopes = (2.0 ** (-8.0 * np.arange(1, A_HEADS + 1) / A_HEADS)).astype(np.float32)
    r, v = np.arange(P)[:, None], np.arange(2 * P)[None, :]
    dist = np.abs(r + v - (P - 1)).astype(np.float32)
    key_chunk = (2 * P - 1 - v) // CHUNK
    query_chunk = 2 + r // CHUNK
    seen = (key_chunk <= query_chunk) & (key_chunk >= query_chunk - 1)
    return np.where(seen[None], -slopes[:, None, None] * dist[None], np.float32(MASKED)).astype(np.float32)


def kernel(**inputs):
    import concourse.bacc as _bacc
    from concourse import mybir as _mybir
    from concourse.bass_utils import run_bass_kernel_spmd as _run

    nc = _bacc.Bacc("TRN2", target_bir_lowering=False, num_devices=1, dynamic_dma_scratch_size=1024)
    arrays, args = {}, []
    consts = {"identity": np.eye(P, dtype=np.float32), "alibi": alibi_strips()}
    for name in [*_INS, *consts]:
        a = np.ascontiguousarray(consts[name] if name in consts else inputs[name])
        arrays[f"in_{name}"] = a
        args.append(nc.dram_tensor(f"in_{name}", a.shape, _mybir.dt.from_np(a.dtype), kind="ExternalInput").ap())
    args.append(nc.dram_tensor("out_0", (1, SEQ, D), F32, kind="ExternalOutput").ap())
    build(nc, *args)
    r = _run(nc, [arrays], core_ids=[0])
    return r.results[0]["out_0"]
```

```python
from contextlib import ExitStack

import numpy as np

import concourse.bass as bass
from concourse import mybir

F32 = mybir.dt.float32
F32R = mybir.dt.float32r
ALU = mybir.AluOpType
ACT = mybir.ActivationFunctionType
AX = mybir.AxisListType

P = 128
D = 2048
SEQ = 512
CHUNK = 64
DH = 64
A_HEADS, A_KV, B_HEADS = 16, 4, 16
HEADS = A_HEADS + B_HEADS
A_WIDTH, A_KVW, B_WIDTH = A_HEADS * DH, A_KV * DH, B_HEADS * DH
REL = 256
D_FF = 4 * D
EPS = 1e-5
MASKED = -1e30
LOWEST = -3.0e38

KB = D // P
TT = SEQ // P
CB = 256
KU = 4
QC = 512
LAND, SPLIT = 4, 2
FC = D_FF // D
CB_CHUNK = D // CB
STRIP = 512
REL_ROW = 640

BLOCKS = ([("k", "a", 0), ("v", "a", 0), ("q", "a", 0), ("q", "a", 1), ("k", "b", 0), ("q", "a", 2),
           ("v", "b", 0), ("q", "a", 3), ("g", "a", 0), ("g", "b", 0), ("q", "b", 0)]
          + [(kind, "b", g) for g in (1, 2, 3) for kind in "qkv"]
          + [("g", "a", 1), ("g", "b", 1)])
COL0 = {("q", "a"): 0, ("k", "a"): A_WIDTH, ("v", "a"): A_WIDTH + A_KVW,
        ("q", "b"): A_WIDTH + 2 * A_KVW, ("k", "b"): A_WIDTH + 2 * A_KVW + B_WIDTH,
        ("v", "b"): A_WIDTH + 2 * A_KVW + 2 * B_WIDTH}
UNITS1 = KU * len(BLOCKS)

SCORES_AT = [13 + 2 * k for k in range(16)] + [46, 48, 51, 53, 56, 59, 62, 65, 68, 71, 74, 76, 78, 81, 83, 85]
TURN_AT = [n + 1 for n in SCORES_AT]
PV_AT = [n + 2 for n in SCORES_AT]
PV_AT[28] = 81


def block_no(kind, mixer, index):
    return BLOCKS.index((kind, mixer, index))


def ready_count(c):
    return sum(kind != "g" for kind, _, _ in BLOCKS[:c + 1])


def slot_of(mixer, g):
    return 1 if mixer == "a" else g % 2


def head_tiles(h):
    out, at = [], 0
    for t in range(TT):
        first = max(0, t - 1) if h < A_HEADS else 0
        n = (t - first + 1) * P
        if h < A_HEADS:
            bank, col = ((4, 0), (4, P), (5, 0), (5, 2 * P))[t]
        else:
            bank, col = ((4, 0), (4, P), (5, 0), (6, 0))[t]
        out.append((first, n, bank, col, at))
        at += n
    return out


def bank_end(h, t):
    tiles = head_tiles(h)
    return max(i for i in range(TT) if tiles[i][2] == tiles[t][2]) + 1


PV_BANK = 7
PROBS = sum(n for _, n, _, _, _ in head_tiles(HEADS - 1))


def build(nc, x, w_in, a_sinks, b_rel_bias, w_branch_a, w_branch_b, w_gate, w_out,
          w_mlp_in, w_mlp_out, norm_final_g, norm_gains, identity_in, alibi_in, out):
    rel_rows = nc.dram_tensor("rel_rows", (B_HEADS, REL_ROW), F32, kind="Internal").ap()

    x_tiles = x[0].rearrange("(t p) d -> p t d", p=P)
    out_tiles = out[0].rearrange("(t p) d -> p t d", p=P)

    def rows(w):
        return w[0].rearrange("(k p) n -> p k n", p=P)

    win, wga, wba, wbb = rows(w_in), rows(w_gate), rows(w_branch_a), rows(w_branch_b)
    wout, wup, wdown = rows(w_out), rows(w_mlp_in), rows(w_mlp_out)

    with ExitStack() as ctx:
        def sb(name, shape, dt=F32, into=ctx):
            return into.enter_context(nc.sbuf_tensor(name, shape, dt))

        def sem(name):
            return ctx.enter_context(nc.semaphore(name))

        bank = ctx.enter_context(nc.psum_tensor("bank", [P, 8, 512], F32))

        landing = sb("landing", [P, LAND, 1024])
        w_hi = sb("w_hi", [P, SPLIT, 1024], F32R)
        w_lo = sb("w_lo", [P, SPLIT, 1024], F32R)
        stream = sb("stream", [P, TT * D])
        xn_hi = sb("xn_hi", [P, KB, SEQ], F32R)
        xn_lo = sb("xn_lo", [P, KB, SEQ], F32R)
        side = sb("side", [P, 4096])
        identity = sb("identity", [P, P])
        gains = sb("gains", [P, 2, KB])
        sinks = sb("sinks", [P, A_HEADS])
        squares = sb("squares", [P, TT, 4])
        stat = sb("stat", [P, 6, TT])
        rms_row = sb("rms_row", [P, SEQ])
        neg_max = sb("neg_max", [P, TT])
        row_max = sb("row_max", [P, TT])
        row_sum = sb("row_sum", [P, TT])
        sink_exp = sb("sink_exp", [P, TT])
        row_inv = sb("row_inv", [P, TT])

        first_phase = ExitStack()
        q_hi = sb("q_hi", [P, 4, SEQ], F32R, first_phase)
        q_lo = sb("q_lo", [P, 4, SEQ], F32R, first_phase)
        k_hi = sb("k_hi", [P, 2, 2, SEQ], F32R, first_phase)
        k_lo = sb("k_lo", [P, 2, 2, SEQ], F32R, first_phase)
        v_parts = sb("v_parts", [P, 2, TT, 4, 2 * DH], F32R, first_phase)
        pt_hi = sb("pt_hi", [P, TT, 512], F32R, first_phase)
        pt_lo = sb("pt_lo", [P, TT, 512], F32R, first_phase)
        probs = sb("probs", [P, PROBS], F32, first_phase)
        strips = sb("strips", [P, 2, STRIP], F32, first_phase)
        from_v_lo = sb("from_v_lo", [P, SEQ], F32, first_phase)
        first_phase.close()
        at_hi = sb("at_hi", [P, KB, SEQ], F32R)
        at_lo = sb("at_lo", [P, KB, SEQ], F32R)
        gain_row = sb("gain_row", [P, D])

        x_tok = stream[:].rearrange("p (t d) -> p t d", t=TT)
        feat = stream[:].rearrange("p (k s) -> p k s", k=KB)
        gate = side[:].rearrange("p (s m b n) -> p s m b n", s=2, m=2, b=2)
        x_again = side[:].rearrange("p (s t n) -> p s t n", s=2, t=TT)
        rms_diagonal = side[:, 3072:3584].rearrange("p (t n) -> p t n", t=TT)
        ones = side[:, 3584:3584 + P]
        scaled = side[:, 2048:4096].rearrange("p (b n) -> p b n", b=4)
        rel_table = side[0:B_HEADS, D:D + REL_ROW]
        relu_z = side[:, 0:1024]
        relu_sq = side[:, 1024:2048]

        def v_part(s, part):
            return v_parts[:, s, :, :, part * DH:(part + 1) * DH].rearrange("p t h d -> p (t h) d")

        def block_parts(c):
            kind, mixer, i = BLOCKS[c]
            if kind == "q" and mixer == "a":
                r = slice((i % 2) * DH, (i % 2 + 1) * DH)
                return scaled[r], q_hi[r], q_lo[r]
            if kind == "q":
                s = slice(2 * (i % 2), 2 * (i % 2) + 2)
                return scaled[:, 0:2, :], q_hi[:, s, :], q_lo[:, s, :]
            s = slot_of(mixer, i)
            if kind == "k":
                return scaled[:, 0:2, :], k_hi[:, s], k_lo[:, s]
            return (scaled[:, 0:2, :].rearrange("p b (t h d) -> p (b t h) d", t=2, h=4),
                    v_part(s, 0), v_part(s, 1))

        x_landed = [sem(f"x_landed{g}") for g in range(4)]
        const_landed = sem("const_landed")
        rel_landed = sem("rel_landed")
        rel_extended = sem("rel_extended")
        rel_stored = sem("rel_stored")
        squared = sem("squared")
        others_squared = sem("others_squared")
        stat_step = sem("stat_step")
        var_ready = sem("var_ready")
        ones_ready = sem("ones_ready")
        root_ready = sem("root_ready")
        diagonal_ready = sem("diagonal_ready")
        row_made = sem("row_made")
        row_ready = sem("row_ready")
        turned = sem("turned")
        norm_hi = sem("norm_hi")
        norm_lo = sem("norm_lo")
        scaled_ready = sem("scaled_ready")
        unit_landed = [sem(f"unit_landed{s}") for s in range(LAND)]
        unit_hi = sem("unit_hi")
        unit_lo = sem("unit_lo")
        unit_used = sem("unit_used")
        proj_hi = sem("proj_hi")
        proj_ready = sem("proj_ready")
        gate_ready = sem("gate_ready")
        strip_landed = [sem("strip_landed0"), sem("strip_landed1")]
        strip_masked = sem("strip_masked")
        scores_done = sem("scores_done")
        biased = sem("biased")
        max_ready = sem("max_ready")
        exp_done = sem("exp_done")
        sum_step = sem("sum_step")
        probs_ready = sem("probs_ready")
        pt_done = sem("pt_done")
        pt_hi_done = sem("pt_hi_done")
        pt_lo_done = sem("pt_lo_done")
        pv_done = sem("pv_done")
        att_lo = sem("att_lo")
        att_ready = sem("att_ready")
        at_hi_done = sem("at_hi_done")
        at_lo_done = sem("at_lo_done")
        branch_a = sem("branch_a")
        branch_b = sem("branch_b")
        merged = sem("merged")
        merged_hi = sem("merged_hi")
        merged_lo = sem("merged_lo")
        x2_landed = [sem("x2_landed0"), sem("x2_landed1")]
        gain3_landed = sem("gain3_landed")
        tile_done = sem("tile_done")
        tile_added = sem("tile_added")
        relu_done = sem("relu_done")
        sq_done = sem("sq_done")
        hidden_hi = sem("hidden_hi")
        hidden_lo = sem("hidden_lo")
        final_ready = sem("final_ready")
        stored = sem("stored")

        B2 = UNITS1 // 4
        LOOP2, PER2 = 3, 6
        B2_END = B2 + LOOP2 * PER2
        B3 = B2_END + 2
        B4 = B3 + 8
        N_BLOCKS1 = len(BLOCKS)
        NBR = D // CB

        SQUARED_X = 4 * 2
        FIRST_PAIRS, PAIRS = (4, 6, 0, 2, 0, 2, 4, 6), (0, 2, 4, 6, 0, 2, 4, 6)
        ROUND = 4 * (TT - 1)

        SPREAD_BANK = 6

        def quad_of(phase3, q):
            return 4 * ((q + 1) % 2) if phase3 else 4 * (q % 2)

        def turned_bank(i, second):
            return quad_of(True, i // 4) + i % 4 if second else 2 + i % 6

        block = ctx.enter_context(nc.Block())

        @block.sync
        def _(sp):
            def load(b, u, src, width):
                s = u % LAND
                if not (isinstance(b, int) and b == 0):
                    sp.wait_ge(unit_lo, 4 * b + (u - LAND + 1))
                dst = landing[:, s, :].rearrange("p (k n) -> p k n", n=width)
                sp.dma_start(dst, src).then_inc(unit_landed[s], 16)

            def load_block(b, w, col, units=4):
                for u in range(units):
                    load(b, u, w[:, KU * u:KU * (u + 1), bass.ds(col, CB)], CB)

            def strip(h):
                if h >= 2:
                    sp.wait_ge(biased, TT * (h - 1))
                if h < A_HEADS:
                    sp.dma_start(strips[:, h % 2, 0:2 * P], alibi_in[h]).then_inc(strip_landed[h % 2], 16)
                else:
                    if h == A_HEADS:
                        sp.wait_ge(rel_stored, 16)
                    row = bass.AP(rel_rows.tensor, (h - A_HEADS) * REL_ROW, [[1, P], [1, STRIP]])
                    sp.dma_start(strips[:, h % 2, :], row).then_inc(strip_landed[h % 2], 16)

            def load_x(g):
                cols = slice(g * QC, (g + 1) * QC)
                sp.dma_start(x_tok[:, :, cols], x_tiles[:, :, cols]).then_inc(x_landed[g], 16)

            load_x(0)
            n = 0
            for c, (kind, mixer, i) in enumerate(BLOCKS):
                if kind == "g":
                    w, col = wga, (0 if mixer == "a" else D) + i * CB
                else:
                    w, col = win, COL0[kind, mixer] + i * CB
                for u in range(KU):
                    load(c, u, w[:, KU * u:KU * (u + 1), col:col + CB], CB)
                    if c == 0 and u < 3:
                        load_x(u + 1)
                    if c == 0 and u == 3:
                        sp.wait_ge(rel_extended, 1)
                        sp.dma_start(rel_rows, rel_table).then_inc(rel_stored, 16)
                        strip(0)
                        strip(1)
                    if n - 6 in SCORES_AT and SCORES_AT.index(n - 6) + 2 < HEADS:
                        strip(SCORES_AT.index(n - 6) + 2)
                    n += 1

            def load_branches(b, nb):
                for u in range(2):
                    load(b, u, wba[:, KU * u:KU * (u + 1), bass.ds(nb * CB, CB)], CB)
                for u in range(2):
                    load(b, 2 + u, wbb[:, KU * u:KU * (u + 1), bass.ds(nb * CB, CB)], CB)

            with sp.Fori(0, LOOP2) as i:
                for j in range(2):
                    b = i * PER2 + (B2 + 3 * j)
                    load_branches(b, i * 2 + j)
                    load_block(b + 1, wga, i * (2 * CB) + (2 + j) * CB)
                    load_block(b + 2, wga, i * (2 * CB) + (D + (2 + j) * CB))
            for j in range(2):
                load_branches(B2_END + j, NBR - 2 + j)

            for q in range(4):
                for u in range(8):
                    cols = slice(q * QC, (q + 1) * QC)
                    load(B3 + 2 * q + u // 4, u % 4, wout[:, 2 * u:2 * u + 2, cols], QC)
                    if u == 5:
                        for r in ((0, 1) if q == 0 else (q + 1,) if q < 3 else ()):
                            if r < 2:
                                sp.wait_ge(merged, NBR)
                            else:
                                sp.wait_ge(tile_added, TT * (r - 1))
                            sp.dma_start(x_again[:, r % 2], x_tiles[:, :, r * QC:(r + 1) * QC])\
                                .then_inc(x2_landed[r % 2], 16)
            def load_up(b, col):
                for j in range(CB_CHUNK):
                    load_block(b + j, wup, col + j * CB)

            def load_down(b, k):
                for q in range(4):
                    for u in range(8):
                        load(b + 2 * q + u // 4, u % 4,
                             wdown[:, bass.ds(k + 2 * u, 2), q * QC:(q + 1) * QC], QC)

            load_up(B4, 0)
            sp.dma_start(gain_row[:], norm_final_g.rearrange("(o d) -> o d", o=1).partition_broadcast(P))\
                .then_inc(gain3_landed, 16)
            with sp.Fori(0, FC - 1) as f:
                load_down(f * 16 + (B4 + 8), f * KB)
                load_up(f * 16 + (B4 + 16), f * D + D)
            last = B4 + 16 * (FC - 1) + 8
            load_down(last, KB * (FC - 1))
            for u in range(8):
                load(last + 8 + u // 4, u % 4, wdown[:, KB * (FC - 1) + 2 * u:KB * (FC - 1) + 2 * u + 2, 3 * QC:], QC)
            for t in range(TT):
                for half in range(2):
                    sp.wait_ge(final_ready, 4 * t + 2 * half + 2)
                    cols = slice(half * D // 2, (half + 1) * D // 2)
                    sp.dma_start(out_tiles[:, t, cols], x_tok[:, t, cols]).then_inc(stored, 16)
            sp.wait_ge(stored, 16 * 2 * TT)

        @block.scalar
        def _(act):
            def split(b, u):
                s = u % SPLIT
                act.wait_ge(unit_landed[u % LAND], 16 * b + 16)
                if not (isinstance(b, int) and 4 * b + u < SPLIT):
                    act.wait_ge(unit_used, 4 * b + (u - SPLIT + 1))
                nc.scalar.activation(w_hi[:, s, :], landing[:, u % LAND, :], ACT.Copy).then_inc(unit_hi, 1)

            def norm_block(i, second, x_hi):
                act.wait_ge(turned, KB * second + i + 1)
                nc.scalar.activation(x_hi[:, i, :], bank[:, turned_bank(i, second), :], ACT.Copy,
                                     scale=gains[:, second, i:i + 1]).then_inc(norm_hi, 1)

            def roots(t0, t1, count):
                act.wait_ge(var_ready, count)
                nc.scalar.activation(stat[:, 2, t0:t1], stat[:, 1, t0:t1], ACT.Sqrt).then_inc(root_ready, 1)

            def rms_to_all(count):
                act.wait_ge(row_made, count)
                nc.scalar.activation(rms_row[:], bank[:, SPREAD_BANK, :], ACT.Copy).then_inc(row_ready, 1)

            def evacuate(c):
                kind, mixer, i = BLOCKS[c]
                act.wait_ge(scaled_ready, c + 1)
                if kind == "g":
                    g = gate[:, i, "ab".index(mixer)]
                    nc.scalar.activation(g, g, ACT.Sigmoid).then_inc(gate_ready, 1)
                    return
                if kind == "q":
                    used = last_scores_before_q(mixer, i)
                    if used:
                        act.wait_ge(scores_done, used)
                elif mixer == "b" and i:
                    if kind == "k":
                        act.wait_ge(scores_done, A_HEADS + 4 * (i - 1))
                    else:
                        act.wait_ge(pv_done, A_HEADS + 4 * (i - 1))
                src, hi, _ = block_parts(c)
                nc.scalar.activation(hi, src, ACT.Copy).then_inc(proj_hi, 1)

            def exponentials(h):
                act.wait_ge(max_ready, h + 1)
                if h < A_HEADS:
                    nc.scalar.activation(sink_exp[:], neg_max[:], ACT.Exp, bias=sinks[:, h:h + 1])
                for t, (_, n, _, _, at) in enumerate(head_tiles(h)):
                    nc.scalar.activation(probs[:, at:at + n], probs[:, at:at + n], ACT.Exp,
                                         bias=neg_max[:, t:t + 1], accum_out=row_sum[:, t:t + 1])\
                        .then_inc(exp_done, 1)

            def turned_probs(h):
                for t, (first, n, bk, col, _) in enumerate(head_tiles(h)):
                    act.wait_ge(pt_done, TT * h + bank_end(h, t))
                    nc.scalar.activation(pt_hi[:, t, first * P:first * P + n], bank[:, bk, col:col + n], ACT.Copy)\
                        .then_inc(pt_hi_done, 1)

            def attended(h):
                act.wait_ge(pv_done, h + 1)
                o = (h % 2) * DH
                if h >= 2:
                    act.wait_ge(att_ready, h - 1)
                nc.scalar.activation(from_v_lo[o:o + DH, :], bank[DH:P, PV_BANK, :], ACT.Copy)\
                    .then_inc(att_lo, 1)

            def stage(n):
                if n in PV_AT:
                    attended(PV_AT.index(n))
                if n in SCORES_AT:
                    exponentials(SCORES_AT.index(n))
                if n in TURN_AT:
                    turned_probs(TURN_AT.index(n))
                if n % KU == KU - 1:
                    evacuate(n // KU)

            act.dma_start(identity[:], identity_in).then_inc(const_landed, 16)
            act.dma_start(gains[:], norm_gains).then_inc(const_landed, 16)
            act.dma_start(rel_table[:, 0:REL + P], b_rel_bias[0, :, REL - P + 1:2 * REL + 1]).then_inc(rel_landed, 16)
            act.dma_start(sinks[:], a_sinks.rearrange("o k g -> o (k g)").partition_broadcast(P))\
                .then_inc(const_landed, 16)

            split(0, 0)
            act.wait_ge(const_landed, 48)
            for i in range(KB):
                norm_block(i, 0, xn_hi)
                g = i // 4
                if i % 4 == 1:
                    act.wait_ge(x_landed[g], 16)
                    for t in (0, 1):
                        k = 2 * g + t
                        if k >= 4:
                            act.wait_ge(squared, k - 3)
                        nc.scalar.activation(pt_hi[:, k % 4, :], x_tok[:, t, g * QC:(g + 1) * QC], ACT.Square,
                                             accum_out=squares[:, t, g:g + 1]).then_inc(squared, 1)
                if i % 4 == 3:
                    split((g + 1) // 4, (g + 1) % 4)
            roots(0, TT, 1)
            rms_to_all(1)

            for n in range(KU + 1, UNITS1):
                split(n // 4, n % 4)
                stage(n - 2)
            split(B2, 0)
            stage(UNITS1 - 2)
            act.wait_ge(scores_done, HEADS)

            def outputs_hi(groups):
                for g in groups:
                    if g == KB // 2 - 1:
                        act.wait_ge(att_ready, HEADS)
                    nc.scalar.activation(at_hi[:, 2 * g:2 * g + 2, :], feat[:, 2 * g:2 * g + 2, :], ACT.Copy)\
                        .then_inc(at_hi_done, 1)

            outputs_hi(range(4))
            split(B2, 1)
            attended(HEADS - 1)
            evacuate(N_BLOCKS1 - 1)
            outputs_hi(range(4, KB // 2))

            def gates(s, m, nb):
                act.wait_ge(scaled_ready, 2 * nb + (m + 1 + N_BLOCKS1 - 4))
                nc.scalar.activation(gate[:, s, m], gate[:, s, m], ACT.Sigmoid).then_inc(gate_ready, 1)

            with act.Fori(0, LOOP2) as i:
                for j in range(2):
                    b = i * PER2 + (B2 + 3 * j)
                    nb = i * 2 + j
                    if j == 1:
                        split(b, 0)
                        split(b, 1)
                        gates(0, 1, nb + 1)
                    split(b, 2)
                    split(b, 3)
                    for u in range(4):
                        split(b + 1, u)
                    split(b + 2, 0)
                    split(b + 2, 1)
                    gates(j, 0, nb + 2)
                    split(b + 2, 2)
                    split(b + 2, 3)
                split(i * PER2 + (B2 + PER2), 0)
                split(i * PER2 + (B2 + PER2), 1)
                gates(1, 1, i * 2 + 3)

            def merged_part(nb):
                act.wait_ge(merged, nb + 1)
                nc.scalar.activation(xn_hi[:, 2 * nb:2 * nb + 2, :], feat[:, 2 * nb:2 * nb + 2, :], ACT.Copy)\
                    .then_inc(merged_hi, 1)

            merged_part(0)
            split(B2_END, 2)
            merged_part(1)
            split(B2_END, 3)
            merged_part(2)
            for u in range(4):
                split(B2_END + 1, u)
                merged_part(3 + u)

            def sum_squares(q, t):
                unused = at_lo[:, TT * q + t, :]
                nc.scalar.activation(unused, x_tok[:, t, q * QC:(q + 1) * QC], ACT.Square,
                                     accum_out=squares[:, t, q:q + 1]).then_inc(squared, 1)

            def out_quarter(b, first_tile, prev, extra=None):
                for u in range(8):
                    split(b + u // 4, u % 4)
                    if u == 1 and extra is not None:
                        extra()
                    if u == 2 and prev is not None:
                        for t in range(TT):
                            act.wait_ge(tile_added, first_tile + t + 1)
                            sum_squares(prev, t)
                    if u in (5, 6) and prev is not None:
                        for i in (0, 1):
                            norm_block(4 * prev + 2 * (u - 5) + i, 1, at_hi)

            def last_tiles(first_tile, t0, t1, count):
                for t in range(t0, t1):
                    act.wait_ge(tile_added, first_tile + 3 * TT + t + 1)
                    sum_squares(3, t)
                roots(t0, t1, count)

            out_quarter(B3, 0, None, lambda: merged_part(NBR - 1))
            for q in range(1, 4):
                out_quarter(B3 + 2 * q, TT * (q - 1), q - 1)
            split(B4, 0)
            split(B4, 1)
            last_tiles(0, 0, TT, 2)
            split(B4, 2)
            for i in range(KB - 4, KB):
                norm_block(i, 1, at_hi)
            split(B4, 3)
            rms_to_all(2)

            def hidden(j, count):
                act.wait_ge(relu_done, count + 1)
                nc.scalar.activation(xn_hi[:, 2 * j:2 * j + 2, :].rearrange("p b n -> p (b n)"), relu_z, ACT.Square)\
                    .then_inc(hidden_hi, 1)

            def up(b, count, started):
                for j in range(1 if started else 0, CB_CHUNK):
                    for u in range(4):
                        split(b + j, u)
                        if u == 1 and j:
                            hidden(j - 1, count + (j - 1))

            def down(b, count):
                for q in range(4):
                    for u in range(8):
                        split(b + 2 * q + u // 4, u % 4)
                        if q == 0 and u == 1:
                            hidden(CB_CHUNK - 1, count + (CB_CHUNK - 1))

            up(B4, 0, True)
            with act.Fori(0, FC - 1) as f:
                down(f * 16 + (B4 + 8), f * CB_CHUNK)
                up(f * 16 + (B4 + 16), f * CB_CHUNK + CB_CHUNK, False)
            last = B4 + 16 * (FC - 1) + 8
            tiles_before = 4 * TT + 4 * TT * (FC - 1)
            for q in range(5):
                for u in range(8):
                    split(last + 2 * q + u // 4, u % 4)
                    if q == 0 and u == 1:
                        hidden(CB_CHUNK - 1, CB_CHUNK * FC - 1)
                    if 0 < q < 4 and u == 2:
                        for t in range(TT):
                            act.wait_ge(tile_added, tiles_before + TT * (q - 1) + t + 1)
                            sum_squares(q - 1, t)
                    if q == 4 and u == 2:
                        last_tiles(tiles_before, 0, 2, 3)
            last_tiles(tiles_before, 2, 4, 4)

        @block.vector
        def _(dve):
            steps = [0]

            def step(ins):
                steps[0] += 1
                ins.then_inc(stat_step, 1)
                dve.wait_ge(stat_step, steps[0])

            def split(b, u):
                s = u % SPLIT
                dve.wait_ge(unit_hi, 4 * b + (u + 1))
                nc.vector.tensor_tensor(w_lo[:, s, :], landing[:, u % LAND, :], w_hi[:, s, :].bitcast(F32),
                                        ALU.subtract).then_inc(unit_lo, 1)

            def inverse_rms(t0, t1, squares_count, roots_count):
                dve.wait_ge(squared, squares_count)
                total, v, root, r, a, c = (stat[:, k, t0:t1] for k in range(6))
                step(nc.vector.tensor_reduce(total, squares[:, t0:t1, :], AX.X, ALU.add))
                nc.vector.tensor_scalar(v, total, 1.0 / D, EPS, ALU.mult, ALU.add).then_inc(var_ready, 1)
                dve.wait_ge(root_ready, roots_count)
                step(nc.vector.reciprocal(r, root))
                step(nc.vector.tensor_tensor(a, r, r, ALU.mult))
                step(nc.vector.tensor_tensor(c, a, v, ALU.mult))
                step(nc.vector.tensor_scalar(a, c, -0.5, 1.5, ALU.mult, ALU.add))
                step(nc.vector.tensor_tensor(c, r, a, ALU.mult))
                return c

            def to_rows(t_inverse):
                shape = [P, TT, P]
                nc.vector.tensor_tensor(rms_diagonal, identity[:].unsqueeze(1).broadcast_to(shape),
                                        t_inverse.unsqueeze(2).broadcast_to(shape), ALU.mult)\
                    .then_inc(diagonal_ready, 1)

            def norm_block(i, second, x_hi, x_lo):
                dve.wait_ge(norm_hi, KB * second + i + 1)
                nc.vector.scalar_tensor_tensor(out=x_lo[:, i, :], in0=bank[:, turned_bank(i, second), :],
                                               scalar=gains[:, second, i:i + 1], in1=x_hi[:, i, :].bitcast(F32),
                                               op0=ALU.mult, op1=ALU.subtract).then_inc(norm_lo, 1)

            def by_token(blocks):
                return rms_row[:].unsqueeze(1).broadcast_to([P, blocks, SEQ])

            def scale(dst, t, g, inverse, gain, done):
                cols = slice(g * QC, (g + 1) * QC)
                nc.vector.scalar_tensor_tensor(out=dst[:, cols], in0=x_tok[:, t, cols], scalar=inverse,
                                               in1=gain[:, cols], op0=ALU.mult, op1=ALU.mult).then_inc(done, 1)

            def scale_block(c):
                kind, mixer, i = BLOCKS[c]
                dve.wait_ge(unit_used, KU * (c + 1))
                if c == 0:
                    dve.wait_ge(row_ready, 1)
                    dve.wait_ge(rel_stored, 16)
                pair = bank[:, 2 * (c % 2):2 * (c % 2) + 2, :]
                if ready_count(c - 1) and (kind != "g" or i == 1):
                    dve.wait_ge(proj_ready, ready_count(c - 1))
                if kind == "g":
                    ins = nc.vector.tensor_tensor(gate[:, i, "ab".index(mixer)], pair, by_token(2), ALU.mult)
                elif kind == "k":
                    ins = nc.vector.tensor_tensor(scaled[:, 0:2, :], pair, by_token(2), ALU.mult)
                elif kind == "v":
                    ins = nc.vector.tensor_tensor(
                        scaled[:, 0:2, :].rearrange("p b (t n) -> p (b t) n", t=2),
                        pair.rearrange("p b (t n) -> p (b t) n", t=2),
                        stat[:, 5, :].unsqueeze(2).broadcast_to([P, TT, CB]), ALU.mult)
                elif mixer == "b":
                    ins = nc.vector.scalar_tensor_tensor(out=scaled[:, 0:2, :], in0=pair, scalar=DH ** -0.5,
                                                         in1=by_token(2), op0=ALU.mult, op1=ALU.mult)
                else:
                    r = (i % 2) * DH
                    for hh in range(4):
                        src = bank[(hh % 2) * DH:(hh % 2 + 1) * DH, 2 * (c % 2) + hh // 2, :]
                        ins = nc.vector.scalar_tensor_tensor(
                            out=scaled[r:r + DH, hh, :], in0=src, scalar=DH ** -0.5,
                            in1=rms_row[r:r + DH, :], op0=ALU.mult, op1=ALU.mult)
                ins.then_inc(scaled_ready, 1)

            def block_lo(c):
                if BLOCKS[c][0] == "g":
                    return
                dve.wait_ge(proj_hi, ready_count(c))
                src, hi, lo = block_parts(c)
                nc.vector.tensor_tensor(lo, src, hi.bitcast(F32), ALU.subtract).then_inc(proj_ready, 1)

            def biased_scores(h):
                s = h % 2
                dve.wait_ge(strip_landed[s], 16 * (h // 2 + 1))
                if h >= A_HEADS:
                    nc.vector.memset(strips[0:CHUNK, s, 0:CHUNK], MASKED).then_inc(strip_masked, 1)
                    dve.wait_ge(strip_masked, h - A_HEADS + 1)
                dve.wait_ge(scores_done, h + 1)
                if h:
                    dve.wait_ge(pt_done, TT * h)
                for t, (_, n, bk, col, at) in enumerate(head_tiles(h)):
                    part = strips[:, s, 0:n]
                    reverse = bass.AP(part.tensor, part.offset + n - 1, [part.ap[0], [-1, n]])
                    nc.vector.tensor_tensor_reduce(
                        out=probs[:, at:at + n], in0=bank[:, bk, col:col + n], in1=reverse, scale=1.0,
                        scalar=LOWEST, op0=ALU.add, op1=ALU.max, accum_out=row_max[:, t:t + 1]).then_inc(biased, 1)
                dve.wait_ge(biased, TT * (h + 1))
                if h < A_HEADS:
                    nc.vector.tensor_scalar(neg_max[:], row_max[:], sinks[:, h:h + 1], -1.0, ALU.max,
                                            ALU.mult).then_inc(max_ready, 1)
                else:
                    nc.vector.tensor_scalar(neg_max[:], row_max[:], -1.0, None, ALU.mult).then_inc(max_ready, 1)

            def attended(h):
                dve.wait_ge(att_lo, h + 1)
                o = (h % 2) * DH
                nc.vector.tensor_tensor(feat[o:o + DH, h // 2, :], bank[0:DH, PV_BANK, :],
                                        from_v_lo[o:o + DH, :], ALU.add).then_inc(att_ready, 1)

            sum_steps = [0]

            def normalise(h):
                dve.wait_ge(exp_done, TT * (h + 1))
                if h < A_HEADS:
                    sum_steps[0] += 1
                    nc.vector.tensor_tensor(row_max[:], row_sum[:], sink_exp[:], ALU.add).then_inc(sum_step, 1)
                    dve.wait_ge(sum_step, sum_steps[0])
                sum_steps[0] += 1
                nc.vector.reciprocal(row_inv[:], row_max[:] if h < A_HEADS else row_sum[:]).then_inc(sum_step, 1)
                dve.wait_ge(sum_step, sum_steps[0])
                for t, (_, n, _, _, at) in enumerate(head_tiles(h)):
                    nc.vector.tensor_scalar(probs[:, at:at + n], probs[:, at:at + n], row_inv[:, t:t + 1], None,
                                            ALU.mult).then_inc(probs_ready, 1)

            def turned_probs(h):
                for t, (first, n, bk, col, _) in enumerate(head_tiles(h)):
                    dve.wait_ge(pt_hi_done, TT * h + bank_end(h, t))
                    nc.vector.tensor_tensor(pt_lo[:, t, first * P:first * P + n], bank[:, bk, col:col + n],
                                            pt_hi[:, t, first * P:first * P + n].bitcast(F32), ALU.subtract)\
                        .then_inc(pt_lo_done, 1)

            nc.vector.memset(ones, 1.0).then_inc(ones_ready, 1)
            dve.wait_ge(rel_landed, 16)
            last = REL + P
            nc.vector.tensor_copy(rel_table[:, last:REL_ROW],
                                  rel_table[:, last - 1:last].broadcast_to([B_HEADS, REL_ROW - last]))\
                .then_inc(rel_extended, 1)

            split(0, 0)
            dve.wait_ge(const_landed, 48)
            for i in range(KB):
                norm_block(i, 0, xn_hi, xn_lo)
                g = i // 4
                if i % 4 == 1:
                    dve.wait_ge(x_landed[g], 16)
                    for t in (2, 3):
                        k = 2 * g + t - 2
                        if k >= 2:
                            dve.wait_ge(others_squared, k - 1)
                        part = x_tok[:, t, g * QC:(g + 1) * QC]
                        nc.vector.tensor_tensor_reduce(
                            out=probs[:, (k % 2) * QC:(k % 2 + 1) * QC], in0=part, in1=part, scale=1.0, scalar=0.0,
                            op0=ALU.mult, op1=ALU.add, accum_out=squares[:, t, g:g + 1]).then_inc(others_squared, 1)
                if i % 4 == 3:
                    split((g + 1) // 4, (g + 1) % 4)
            dve.wait_ge(others_squared, 8)
            to_rows(inverse_rms(0, TT, SQUARED_X, 1))

            for n in range(KU + 1, UNITS1 + 1):
                m = n - 2
                head = SCORES_AT.index(m) if m in SCORES_AT else None
                if head is not None:
                    biased_scores(head)
                split(n // 4, n % 4)
                if m in TURN_AT:
                    turned_probs(TURN_AT.index(m))
                if m in PV_AT:
                    attended(PV_AT.index(m))
                if head is not None:
                    normalise(head)
                if m % KU == KU - 1:
                    scale_block(m // KU)
                if m % KU == 0:
                    block_lo(m // KU - 1)
            split(B2, 1)
            scale_block(N_BLOCKS1 - 1)
            dve.wait_ge(pv_done, HEADS)
            for g in range(KB // 2):
                if g == 2:
                    attended(HEADS - 1)
                dve.wait_ge(at_hi_done, g + 1)
                nc.vector.tensor_tensor(at_lo[:, 2 * g:2 * g + 2, :], feat[:, 2 * g:2 * g + 2, :],
                                        at_hi[:, 2 * g:2 * g + 2, :].bitcast(F32), ALU.subtract)\
                    .then_inc(at_lo_done, 1)

            def scaled_a(b, s, nb):
                dve.wait_ge(unit_used, 4 * b + 2)
                dve.wait_ge(gate_ready, 2 * nb + 2)
                nc.vector.tensor_tensor(feat[:, bass.ds(2 * nb, 2), :], gate[:, s, 0], bank[:, 0:2, :], ALU.mult)\
                    .then_inc(branch_a, 1)

            def merge_b(b, s, nb):
                dve.wait_ge(unit_used, 4 * b + 4)
                nc.vector.tensor_tensor(gate[:, s, 1], gate[:, s, 1], bank[:, 2:4, :], ALU.mult)\
                    .then_inc(branch_b, 1)
                dve.wait_ge(branch_a, nb + 1)
                dve.wait_ge(branch_b, nb + 1)
                nc.vector.tensor_tensor(feat[:, bass.ds(2 * nb, 2), :], feat[:, bass.ds(2 * nb, 2), :],
                                        gate[:, s, 1], ALU.add).then_inc(merged, 1)

            def gate_logits(b, s, m, nb):
                dve.wait_ge(unit_used, 4 * b + 4)
                dve.wait_ge(merged, nb - 1)
                nc.vector.tensor_tensor(gate[:, s, m], bank[:, 2 * m:2 * m + 2, :], by_token(2), ALU.mult)\
                    .then_inc(scaled_ready, 1)

            with dve.Fori(0, LOOP2) as i:
                for j in range(2):
                    b = i * PER2 + (B2 + 3 * j)
                    nb = i * 2 + j
                    if j == 1:
                        split(b, 0)
                        split(b, 1)
                        gate_logits(b - 1, 0, 1, nb + 1)
                    split(b, 2)
                    split(b, 3)
                    scaled_a(b, j, nb)
                    split(b + 1, 0)
                    split(b + 1, 1)
                    merge_b(b, j, nb)
                    split(b + 1, 2)
                    split(b + 1, 3)
                    split(b + 2, 0)
                    split(b + 2, 1)
                    gate_logits(b + 1, j, 0, nb + 2)
                    split(b + 2, 2)
                    split(b + 2, 3)
                split(i * PER2 + (B2 + PER2), 0)
                split(i * PER2 + (B2 + PER2), 1)
                gate_logits(i * PER2 + (B2 + PER2 - 1), 1, 1, i * 2 + 3)

            def merged_part(nb):
                dve.wait_ge(merged_hi, nb + 1)
                nc.vector.tensor_tensor(xn_lo[:, 2 * nb:2 * nb + 2, :], feat[:, 2 * nb:2 * nb + 2, :],
                                        xn_hi[:, 2 * nb:2 * nb + 2, :].bitcast(F32), ALU.subtract)\
                    .then_inc(merged_lo, 1)

            merged_part(0)
            split(B2_END, 2)
            merged_part(1)
            split(B2_END, 3)
            scaled_a(B2_END, 0, NBR - 2)
            merged_part(2)
            for u in range(4):
                split(B2_END + 1, u)
                if u == 1:
                    merge_b(B2_END, 0, NBR - 2)
                if u == 3:
                    scaled_a(B2_END + 1, 1, NBR - 1)
                merged_part(3 + u)

            def tile_complete(k, tiles, before, b):
                if k < tiles - 1:
                    dve.wait_ge(tile_done, before + (k + 1))
                else:
                    dve.wait_ge(unit_used, 4 * b + 8)

            def residual(q, t, before, b):
                tile_complete(t, TT, before, b)
                add_tile(q, t)

            def add_tile(q, t):
                dst = x_tok[:, t, q * QC:(q + 1) * QC]
                nc.vector.tensor_tensor(dst, dst, bank[:, quad_of(False, q) + t, :], ALU.add)\
                    .then_inc(tile_added, 1)

            def residual3(q):
                dve.wait_ge(x2_landed[q % 2], 16 * (q // 2 + 1))
                for t in range(TT):
                    tile_complete(t, TT, (TT - 1) * q, B3 + 2 * q)
                    nc.vector.tensor_tensor(x_tok[:, t, q * QC:(q + 1) * QC], x_again[:, q % 2, t, :],
                                            bank[:, quad_of(True, q) + t, :], ALU.add).then_inc(tile_added, 1)

            for q in range(4):
                for u in range(8):
                    split(B3 + 2 * q + u // 4, u % 4)
                    if q == 0 and u == 1:
                        merge_b(B2_END + 1, 1, NBR - 1)
                        merged_part(NBR - 1)
                    if q > 0 and u == 1:
                        residual3(q - 1)
                    if q > 0 and u in (5, 6):
                        for i in (0, 1):
                            norm_block(4 * (q - 1) + 2 * (u - 5) + i, 1, at_hi, at_lo)

            split(B4, 0)
            split(B4, 1)
            residual3(3)
            dve.wait_ge(tile_added, 4 * TT)
            nc.vector.memset(ones, 1.0).then_inc(ones_ready, 1)
            to_rows(inverse_rms(0, TT, SQUARED_X + 16, 2))
            split(B4, 2)
            for i in range(KB - 4, KB):
                norm_block(i, 1, at_hi, at_lo)
            split(B4, 3)

            def hidden(b, j, pair, count):
                dve.wait_ge(unit_used, 4 * b + 4)
                if j == 0:
                    dve.wait_ge(row_ready, 2)
                relu_pair, square_pair = (buf.rearrange("p (b n) -> p b n", b=2) for buf in (relu_z, relu_sq))
                nc.vector.scalar_tensor_tensor(out=relu_pair, in0=bank[:, pair:pair + 2, :], scalar=0.0,
                                               in1=by_token(2), op0=ALU.max, op1=ALU.mult).then_inc(relu_done, 1)
                dve.wait_ge(relu_done, count + 1)
                nc.vector.tensor_tensor(square_pair, relu_pair, relu_pair, ALU.mult).then_inc(sq_done, 1)
                dve.wait_ge(sq_done, count + 1)
                dve.wait_ge(hidden_hi, count + 1)
                nc.vector.tensor_tensor(xn_lo[:, 2 * j:2 * j + 2, :], square_pair,
                                        xn_hi[:, 2 * j:2 * j + 2, :].bitcast(F32), ALU.subtract)\
                    .then_inc(hidden_lo, 1)

            def up(b, count, started, before):
                for j in range(1 if started else 0, CB_CHUNK):
                    for u in range(4):
                        split(b + j, u)
                        if u == 1 and j:
                            hidden(b + j - 1, j - 1, (FIRST_PAIRS if started else PAIRS)[j - 1], count + (j - 1))
                        if u == 1 and not j and before is not None:
                            for t in range(TT):
                                residual(3, t, before + 3 * (TT - 1), b - 2)

            def down(b, count, before):
                for q in range(4):
                    for u in range(8):
                        split(b + 2 * q + u // 4, u % 4)
                        if q == 0 and u == 1:
                            hidden(b - 1, CB_CHUNK - 1, 6, count + (CB_CHUNK - 1))
                        if q > 0 and u == 1:
                            for t in range(TT):
                                residual(q - 1, t, before + (TT - 1) * (q - 1), b + 2 * (q - 1))

            up(B4, 0, True, None)
            with dve.Fori(0, FC - 1) as f:
                down(f * 16 + (B4 + 8), f * CB_CHUNK, f * ROUND + ROUND)
                up(f * 16 + (B4 + 16), f * CB_CHUNK + CB_CHUNK, False, f * ROUND + ROUND)
            last = B4 + 16 * (FC - 1) + 8
            before = ROUND * FC
            down(last, CB_CHUNK * (FC - 1), before)

            def finish(t, gs, c):
                for g in gs:
                    scale(x_tok[:, t, :], t, g, c, gain_row, final_ready)

            for u in range(8):
                split(last + 8 + u // 4, u % 4)
                if u == 1:
                    for t in (0, 1):
                        tile_complete(t, 2, before + 3 * (TT - 1), last + 6)
                        add_tile(3, t)
                if u == 2:
                    c = inverse_rms(0, 2, SQUARED_X + 16 + 14, 3)
                    dve.wait_ge(gain3_landed, 16)
                if u in (3, 4, 5, 6):
                    finish((u - 3) // 2, (0, 1) if u % 2 else (2, 3), c[:, (u - 3) // 2:(u - 3) // 2 + 1])
            for t in (2, 3):
                tile_complete(t - 2, 2, before + 3 * (TT - 1) + 1, last + 8)
                add_tile(3, t)
            c = inverse_rms(2, 4, SQUARED_X + 16 + 16, 4)
            for t in (2, 3):
                finish(t, range(4), c[:, t - 2:t - 1])

        @block.tensor
        def _(pe):
            def product(dst, a_hi, a_lo, b_hi, b_lo, start, stop, **kw):
                nc.tensor.matmul(dst, a_hi, b_hi, start=start, stop=False, **kw)
                nc.tensor.matmul(dst, a_hi, b_lo, start=False, stop=False, **kw)
                return nc.tensor.matmul(dst, a_lo, b_hi, start=False, stop=stop, **kw)

            def turn(i, second):
                for t in range(TT):
                    ins = nc.tensor.transpose(bank[:, turned_bank(i, second), t * P:(t + 1) * P],
                                              x_tok[:, t, i * P:(i + 1) * P], identity[:])
                ins.then_inc(turned, 1)

            def spread_rms(second):
                pe.wait_ge(ones_ready, second + 1)
                pe.wait_ge(diagonal_ready, second + 1)
                nc.tensor.matmul(bank[:, SPREAD_BANK, :], ones, rms_diagonal.rearrange("p t n -> p (t n)"),
                                 start=True, stop=True).then_inc(row_made, 1)

            def turn_x(i):
                if i % 4 == 0:
                    pe.wait_ge(x_landed[i // 4], 16)
                if i >= 6:
                    pe.wait_ge(norm_lo, i - 5)
                turn(i, 0)

            def first_block():
                for u in range(KU):
                    pe.wait_ge(unit_lo, u + 1)
                    s = u % SPLIT
                    wh = w_hi[:, s, :].rearrange("p (k n) -> p k n", n=CB)
                    wl = w_lo[:, s, :].rearrange("p (k n) -> p k n", n=CB)
                    for k in range(KU):
                        i = KU * u + k
                        if i + 3 < KB:
                            turn_x(i + 3)
                        pe.wait_ge(norm_lo, i + 1)
                        for nb in range(2):
                            cols = slice(nb * P, (nb + 1) * P)
                            ins = product(bank[:, nb, :], wh[:, k, cols], wl[:, k, cols], xn_hi[:, i, :],
                                          xn_lo[:, i, :], i == 0, i == KB - 1)
                    ins.then_inc(unit_used, 1)

            def features(b, u, pair, k0, first, last, x_hi, x_lo):
                pe.wait_ge(unit_lo, 4 * b + (u + 1))
                s = u % SPLIT
                wh = w_hi[:, s, :].rearrange("p (k n) -> p k n", n=CB)
                wl = w_lo[:, s, :].rearrange("p (k n) -> p k n", n=CB)
                for nb in range(2):
                    for k in range(KU):
                        cols = slice(nb * P, (nb + 1) * P)
                        ins = product(bank[:, pair + nb, :], wh[:, k, cols], wl[:, k, cols],
                                      x_hi[:, k0 + k, :], x_lo[:, k0 + k, :],
                                      first and k == 0, last and k == KU - 1)
                ins.then_inc(unit_used, 1)

            def values(b, u, pair):
                pe.wait_ge(unit_lo, 4 * b + (u + 1))
                s = u % SPLIT
                wh = w_hi[:, s, :].rearrange("p (k n) -> p k n", n=CB)
                wl = w_lo[:, s, :].rearrange("p (k n) -> p k n", n=CB)
                for k in range(KU):
                    for t in range(TT):
                        cols = slice(t * P, (t + 1) * P)
                        kb = KU * u + k
                        dst = bank[:, pair + t // 2, (t % 2) * CB:(t % 2 + 1) * CB]
                        ins = product(dst, xn_hi[:, kb, cols], xn_lo[:, kb, cols], wh[:, k, :], wl[:, k, :],
                                      kb == 0 and t % 2 == 0, kb == KB - 1, skip_group_check=True)
                ins.then_inc(unit_used, 1)

            def scores(h):
                mixer, g = ("a", h // 4) if h < A_HEADS else ("b", (h - A_HEADS) // 4)
                hh = h % 4
                if h:
                    pe.wait_ge(pt_lo_done, TT * h)
                pe.wait_ge(proj_ready, max(ready_count(block_no(kind, mixer, g if kind == "q" or mixer == "b" else 0))
                                           for kind in "qk"))
                if mixer == "a":
                    r, qb, kb = (g % 2) * DH, hh, g // 2
                else:
                    r, qb, kb = (hh % 2) * DH, 2 * (g % 2) + hh // 2, hh // 2
                s = slot_of(mixer, g)
                for t, (first, n, bk, col, _) in enumerate(head_tiles(h)):
                    qs, ks = slice(t * P, (t + 1) * P), slice(first * P, first * P + n)
                    ins = product(bank[:, bk, col:col + n], q_hi[r:r + DH, qb, qs], q_lo[r:r + DH, qb, qs],
                                  k_hi[r:r + DH, s, kb, ks], k_lo[r:r + DH, s, kb, ks], True, True)
                ins.then_inc(scores_done, 1)

            def turn_probs(h):
                for t, (_, n, bk, col, at) in enumerate(head_tiles(h)):
                    pe.wait_ge(probs_ready, TT * h + t + 1)
                    for k in range(n // P):
                        ins = nc.tensor.transpose(bank[:, bk, col + k * P:col + (k + 1) * P],
                                                  probs[:, at + k * P:at + (k + 1) * P], identity[:])
                    ins.then_inc(pt_done, 1)

            def times_v(h):
                mixer, g = ("a", 0) if h < A_HEADS else ("b", (h - A_HEADS) // 4)
                head = h // 4 if h < A_HEADS else h % 4
                s = slot_of(mixer, g)
                pe.wait_ge(proj_ready, ready_count(block_no("v", mixer, g)))
                pe.wait_ge(pt_lo_done, TT * (h + 1))
                if h:
                    pe.wait_ge(att_ready, h)
                for j in range(TT):
                    last = min(j + 2, TT) if h < A_HEADS else TT
                    dst = bank[:, PV_BANK, j * P:last * P].rearrange("p (t q) -> p t q", q=P)
                    for part in (pt_hi, pt_lo):
                        ins = nc.tensor.matmul(dst, v_parts[:, s, j, head, :],
                                               part[:, j:last, j * P:(j + 1) * P],
                                               start=j == 0 and part is pt_hi,
                                               stop=j == TT - 1 and part is pt_lo, skip_group_check=True)
                ins.then_inc(pv_done, 1)

            pe.wait_ge(const_landed, 48)
            for i in range(3):
                turn_x(i)
            first_block()
            spread_rms(0)

            for n in range(KU, UNITS1):
                c, u = n // KU, n % KU
                kind, _, _ = BLOCKS[c]
                if u == 0 and c >= 2:
                    pe.wait_ge(scaled_ready, c - 1)
                if kind == "v":
                    values(c, u, 2 * (c % 2))
                else:
                    features(c, u, 2 * (c % 2), KU * u, u == 0, u == KU - 1, xn_hi, xn_lo)
                if n in PV_AT:
                    times_v(PV_AT.index(n))
                if n in SCORES_AT:
                    scores(SCORES_AT.index(n))
                if n in TURN_AT:
                    turn_probs(TURN_AT.index(n))

            def branches(b, nb):
                pe.wait_ge(scaled_ready, 2 * nb + (N_BLOCKS1 - 1))
                for u in range(2):
                    pe.wait_ge(at_lo_done, 2 * u + 2)
                    features(b, u, 0, KU * u, u == 0, u == 1, at_hi, at_lo)
                pe.wait_ge(scaled_ready, 2 * nb + N_BLOCKS1)
                for u in range(2):
                    pe.wait_ge(at_lo_done, 2 * u + 6)
                    features(b, 2 + u, 2, KB // 2 + KU * u, u == 0, u == 1, at_hi, at_lo)

            def gate_block(b, pair, left):
                pe.wait_ge(branch_b if pair else branch_a, left)
                for u in range(4):
                    features(b, u, 2 * pair, KU * u, u == 0, u == 3, xn_hi, xn_lo)

            with pe.Fori(0, LOOP2) as i:
                for j in range(2):
                    b = i * PER2 + (B2 + 3 * j)
                    nb = i * 2 + j
                    branches(b, nb)
                    gate_block(b + 1, 0, nb + 1)
                    gate_block(b + 2, 1, nb + 1)
            branches(B2_END, NBR - 2)
            pe.wait_ge(branch_a, NBR - 1)
            for u in range(2):
                features(B2_END + 1, u, 0, KU * u, u == 0, u == 1, at_hi, at_lo)
            pe.wait_ge(branch_b, NBR - 1)
            for u in range(2):
                features(B2_END + 1, 2 + u, 2, KB // 2 + KU * u, u == 0, u == 1, at_hi, at_lo)

            def quarter(b, first_bank, before, x_hi, x_lo, ready=None, tiles=range(TT), after=None):
                for u in range(8):
                    pe.wait_ge(unit_lo, 4 * b + (u + 1))
                    s = u % SPLIT
                    wh = w_hi[:, s, :].rearrange("p (k n) -> p k n", n=QC)
                    wl = w_lo[:, s, :].rearrange("p (k n) -> p k n", n=QC)
                    if ready is not None:
                        ready(u)
                    for k in range(2):
                        kb = 2 * u + k
                        for t in tiles:
                            if kb == 0:
                                before(t)
                            cols = slice(t * P, (t + 1) * P)
                            ins = product(bank[:, first_bank + t, :], x_hi[:, kb, cols], x_lo[:, kb, cols],
                                          wh[:, k, :], wl[:, k, :], kb == 0, kb == KB - 1)
                            if kb == KB - 1 and t != tiles[-1]:
                                ins.then_inc(tile_done, 1)
                    ins.then_inc(unit_used, 1)
                    if after is not None:
                        after(u)

            def before3(q):
                def wait(t):
                    if q == 0 and t == 0:
                        pe.wait_ge(att_ready, HEADS)
                    if q == 1 and t == 0:
                        pe.wait_ge(branch_b, NBR)
                    if q >= 2:
                        pe.wait_ge(norm_lo, KB + 4 * (q - 2) + t + 1)
                return wait

            def turn_quarter(q):
                pe.wait_ge(tile_added, TT * (q + 1))
                for i in range(4 * q, 4 * q + 4):
                    turn(i, 1)

            for q in range(4):
                quarter(B3 + 2 * q, quad_of(True, q), before3(q), xn_hi, xn_lo,
                        (lambda u: pe.wait_ge(merged_lo, u + 1)) if q == 0 else None,
                        after=(lambda u, q=q: turn_quarter(q - 1) if u == 3 else None) if q else None)
            for u in range(KU):
                pe.wait_ge(norm_lo, KB + KU * (u + 1))
                if u == 0:
                    pe.wait_ge(norm_lo, KB + 10)
                features(B4, u, FIRST_PAIRS[0], KU * u, u == 0, u == 3, at_hi, at_lo)
                if u == 0:
                    turn_quarter(3)
                if u == 1:
                    pe.wait_ge(norm_lo, KB + 12)
                    spread_rms(1)

            def up(b, count, tiles):
                for j in range(0 if tiles is not None else 1, CB_CHUNK):
                    if tiles is None and j >= 4:
                        pe.wait_ge(relu_done, (3, 4, 1, 2)[j - 4])
                    elif j >= 4:
                        pe.wait_ge(relu_done, count + (j - 3))
                    elif tiles is not None:
                        pe.wait_ge(tile_added, tiles + 2 * TT + 2 * j + 2)
                    elif j == 1:
                        pe.wait_ge(row_ready, 2)
                    for u in range(4):
                        features(b + j, u, (PAIRS if tiles is not None else FIRST_PAIRS)[j], KU * u, u == 0, u == 3, at_hi, at_lo)

            def down(b, count, tiles, quarters=range(4)):
                for q in quarters:
                    def before(t, q=q):
                        if q < 2 and t % 2 == 0:
                            pe.wait_ge(relu_done, count + (5 + 2 * q + t // 2))
                        if q >= 2:
                            pe.wait_ge(tile_added, tiles + (TT * (q - 2) + t + 1))

                    def ready(u):
                        pe.wait_ge(hidden_lo, count + (u + 1))

                    quarter(b + 2 * q, quad_of(False, q), before, xn_hi, xn_lo, ready if q == 0 else None)

            up(B4, 0, None)
            with pe.Fori(0, FC - 1) as f:
                tiles = f * (4 * TT) + 4 * TT
                down(f * 16 + (B4 + 8), f * CB_CHUNK, tiles)
                up(f * 16 + (B4 + 16), f * CB_CHUNK + CB_CHUNK, tiles)
            last = B4 + 16 * (FC - 1) + 8
            down(last, CB_CHUNK * (FC - 1), 4 * TT * FC, range(3))

            def before_last(t):
                pe.wait_ge(tile_added, 4 * TT * FC + TT + t + 1)

            quarter(last + 6, quad_of(False, 3), before_last, xn_hi, xn_lo, None, (0, 1))
            quarter(last + 8, quad_of(False, 3), before_last, xn_hi, xn_lo, None, (2, 3))


def last_scores_before_q(mixer, i):
    if mixer == "a":
        return 4 * (i - 1) if i >= 2 else 0
    return A_HEADS if i == 0 else A_HEADS if i == 1 else A_HEADS + 4 * (i - 1)


_INS = ["x", "w_in", "a_sinks", "b_rel_bias", "w_branch_a", "w_branch_b", "w_gate",
        "w_out", "w_mlp_in", "w_mlp_out", "norm_final_g"]


def alibi_strips():
    slopes = (2.0 ** (-8.0 * np.arange(1, A_HEADS + 1) / A_HEADS)).astype(np.float32)
    r, v = np.arange(P)[:, None], np.arange(2 * P)[None, :]
    dist = np.abs(r + v - (P - 1)).astype(np.float32)
    key_chunk = (2 * P - 1 - v) // CHUNK
    query_chunk = 2 + r // CHUNK
    seen = (key_chunk <= query_chunk) & (key_chunk >= query_chunk - 1)
    return np.where(seen[None], -slopes[:, None, None] * dist[None], np.float32(MASKED)).astype(np.float32)


def kernel(**inputs):
    import concourse.bacc as _bacc
    from concourse import mybir as _mybir
    from concourse.bass_utils import run_bass_kernel_spmd as _run

    nc = _bacc.Bacc("TRN2", target_bir_lowering=False, num_devices=1, dynamic_dma_scratch_size=1024)
    arrays, args = {}, []
    norm_gains = np.stack([inputs[name].reshape(KB, P).T for name in ("norm_mix_g", "norm_mlp_g")], axis=1)
    others = {"norm_gains": norm_gains, "identity": np.eye(P, dtype=np.float32), "alibi": alibi_strips()}
    for name in [*_INS, *others]:
        a = np.ascontiguousarray(others[name] if name in others else inputs[name])
        arrays[f"in_{name}"] = a
        args.append(nc.dram_tensor(f"in_{name}", a.shape, _mybir.dt.from_np(a.dtype), kind="ExternalInput").ap())
    args.append(nc.dram_tensor("out_0", (1, SEQ, D), F32, kind="ExternalOutput").ap())
    build(nc, *args)
    r = _run(nc, [arrays], core_ids=[0])
    return r.results[0]["out_0"]
```

```python
from contextlib import ExitStack

import numpy as np

import concourse.bass as bass
from concourse import mybir

F32 = mybir.dt.float32
F32R = mybir.dt.float32r
ALU = mybir.AluOpType
ACT = mybir.ActivationFunctionType
AX = mybir.AxisListType

P = 128
D = 2048
SEQ = 512
CHUNK = 64
DH = 64
A_HEADS, A_KV, B_HEADS = 16, 4, 16
HEADS = A_HEADS + B_HEADS
A_WIDTH, A_KVW, B_WIDTH = A_HEADS * DH, A_KV * DH, B_HEADS * DH
REL = 256
D_FF = 4 * D
EPS = 1e-5
MASKED = -1e30
LOWEST = -3.0e38

KB = D // P
TT = SEQ // P
CB = 256
KU = 4
QC = 512
LAND, SPLIT = 4, 2
FC = D_FF // D
CB_CHUNK = D // CB
STRIP = 512
REL_ROW = 640

BLOCKS = ([("k", "a", 0), ("v", "a", 0), ("q", "a", 0), ("q", "a", 1), ("k", "b", 0), ("q", "a", 2),
           ("v", "b", 0), ("q", "a", 3), ("g", "a", 0), ("g", "b", 0), ("q", "b", 0)]
          + [(kind, "b", g) for g in (1, 2, 3) for kind in "qkv"]
          + [("g", "a", 1), ("g", "b", 1)])
COL0 = {("q", "a"): 0, ("k", "a"): A_WIDTH, ("v", "a"): A_WIDTH + A_KVW,
        ("q", "b"): A_WIDTH + 2 * A_KVW, ("k", "b"): A_WIDTH + 2 * A_KVW + B_WIDTH,
        ("v", "b"): A_WIDTH + 2 * A_KVW + 2 * B_WIDTH}
UNITS1 = KU * len(BLOCKS)

SCORES_AT = [13 + 2 * k for k in range(16)] + [46, 48, 51, 53, 56, 59, 62, 65, 68, 71, 74, 76, 78, 81, 83, 85]
TURN_AT = [n + 1 for n in SCORES_AT]
PV_AT = [n + 2 for n in SCORES_AT]
PV_AT[28] = 81


def block_no(kind, mixer, index):
    return BLOCKS.index((kind, mixer, index))


def ready_count(c):
    return sum(kind != "g" for kind, _, _ in BLOCKS[:c + 1])


def slot_of(mixer, g):
    return 1 if mixer == "a" else g % 2


def head_tiles(h):
    out, at = [], 0
    for t in range(TT):
        first = max(0, t - 1) if h < A_HEADS else 0
        n = (t - first + 1) * P
        if h < A_HEADS:
            bank, col = ((4, 0), (4, P), (5, 0), (5, 2 * P))[t]
        else:
            bank, col = ((4, 0), (4, P), (5, 0), (6, 0))[t]
        out.append((first, n, bank, col, at))
        at += n
    return out


def bank_end(h, t):
    tiles = head_tiles(h)
    return max(i for i in range(TT) if tiles[i][2] == tiles[t][2]) + 1


PV_BANK = 7
PROBS = sum(n for _, n, _, _, _ in head_tiles(HEADS - 1))


def build(nc, x, w_in, a_sinks, b_rel_bias, w_branch_a, w_branch_b, w_gate, w_out,
          w_mlp_in, w_mlp_out, norm_final_g, x_features, norm_gains, identity_in, alibi_in, out):
    rel_rows = nc.dram_tensor("rel_rows", (B_HEADS, REL_ROW), F32, kind="Internal").ap()

    x_tiles = x[0].rearrange("(t p) d -> p t d", p=P)
    x_blocks = x_features.rearrange("(k p) s -> p k s", p=P)
    out_tiles = out[0].rearrange("(t p) d -> p t d", p=P)

    def rows(w):
        return w[0].rearrange("(k p) n -> p k n", p=P)

    win, wga, wba, wbb = rows(w_in), rows(w_gate), rows(w_branch_a), rows(w_branch_b)
    wout, wup, wdown = rows(w_out), rows(w_mlp_in), rows(w_mlp_out)

    with ExitStack() as ctx:
        def sb(name, shape, dt=F32, into=ctx):
            return into.enter_context(nc.sbuf_tensor(name, shape, dt))

        def sem(name):
            return ctx.enter_context(nc.semaphore(name))

        bank = ctx.enter_context(nc.psum_tensor("bank", [P, 8, 512], F32))

        landing = sb("landing", [P, LAND, 1024])
        w_hi = sb("w_hi", [P, SPLIT, 1024], F32R)
        w_lo = sb("w_lo", [P, SPLIT, 1024], F32R)
        stream = sb("stream", [P, TT * D])
        xn_hi = sb("xn_hi", [P, KB, SEQ], F32R)
        xn_lo = sb("xn_lo", [P, KB, SEQ], F32R)
        side = sb("side", [P, 4096])
        identity = sb("identity", [P, P])
        gains = sb("gains", [P, 2, KB])
        sinks = sb("sinks", [P, A_HEADS])
        squares = sb("squares", [P, TT, 4])
        stat = sb("stat", [P, 6, TT])
        rms_row = sb("rms_row", [P, SEQ])
        neg_max = sb("neg_max", [P, TT])
        row_max = sb("row_max", [P, TT])
        row_sum = sb("row_sum", [P, TT])
        sink_exp = sb("sink_exp", [P, TT])
        row_inv = sb("row_inv", [P, TT])

        prologue = ExitStack()
        x_rows = sb("x_rows", [P, TT, D], F32, prologue)
        prologue.close()
        first_phase = ExitStack()
        q_hi = sb("q_hi", [P, 4, SEQ], F32R, first_phase)
        q_lo = sb("q_lo", [P, 4, SEQ], F32R, first_phase)
        k_hi = sb("k_hi", [P, 2, 2, SEQ], F32R, first_phase)
        k_lo = sb("k_lo", [P, 2, 2, SEQ], F32R, first_phase)
        v_parts = sb("v_parts", [P, 2, TT, 4, 2 * DH], F32R, first_phase)
        pt_hi = sb("pt_hi", [P, TT, 512], F32R, first_phase)
        pt_lo = sb("pt_lo", [P, TT, 512], F32R, first_phase)
        probs = sb("probs", [P, PROBS], F32, first_phase)
        strips = sb("strips", [P, 2, STRIP], F32, first_phase)
        from_v_lo = sb("from_v_lo", [P, SEQ], F32, first_phase)
        first_phase.close()
        at_hi = sb("at_hi", [P, KB, SEQ], F32R)
        at_lo = sb("at_lo", [P, KB, SEQ], F32R)
        gain_row = sb("gain_row", [P, D])

        x_tok = stream[:].rearrange("p (t d) -> p t d", t=TT)
        feat = stream[:].rearrange("p (k s) -> p k s", k=KB)
        gate = side[:].rearrange("p (s m b n) -> p s m b n", s=2, m=2, b=2)
        x_again = side[:].rearrange("p (s t n) -> p s t n", s=2, t=TT)
        rms_diagonal = side[:, 3072:3584].rearrange("p (t n) -> p t n", t=TT)
        ones = side[:, 3584:3584 + P]
        scaled = side[:, 2048:4096].rearrange("p (b n) -> p b n", b=4)
        rel_table = side[0:B_HEADS, D:D + REL_ROW]
        relu_z = side[:, 0:1024]
        relu_sq = side[:, 1024:2048]

        def v_part(s, part):
            return v_parts[:, s, :, :, part * DH:(part + 1) * DH].rearrange("p t h d -> p (t h) d")

        def block_parts(c):
            kind, mixer, i = BLOCKS[c]
            if kind == "q" and mixer == "a":
                r = slice((i % 2) * DH, (i % 2 + 1) * DH)
                return scaled[r], q_hi[r], q_lo[r]
            if kind == "q":
                s = slice(2 * (i % 2), 2 * (i % 2) + 2)
                return scaled[:, 0:2, :], q_hi[:, s, :], q_lo[:, s, :]
            s = slot_of(mixer, i)
            if kind == "k":
                return scaled[:, 0:2, :], k_hi[:, s], k_lo[:, s]
            return (scaled[:, 0:2, :].rearrange("p b (t h d) -> p (b t h) d", t=2, h=4),
                    v_part(s, 0), v_part(s, 1))

        x_landed = [sem(f"x_landed{g}") for g in range(4)]
        rows_landed = [sem(f"rows_landed{t}") for t in range(TT)]
        gains_landed = sem("gains_landed")
        const_landed = sem("const_landed")
        x_start_landed = sem("x_start_landed")
        sinks_landed = sem("sinks_landed")
        rel_landed = sem("rel_landed")
        rel_extended = sem("rel_extended")
        rel_stored = sem("rel_stored")
        squared = sem("squared")
        others_squared = sem("others_squared")
        stat_step = sem("stat_step")
        var_ready = sem("var_ready")
        ones_ready = sem("ones_ready")
        root_ready = sem("root_ready")
        inverse_ready = sem("inverse_ready")
        gained = sem("gained")
        diagonal_ready = sem("diagonal_ready")
        row_made = sem("row_made")
        row_ready = sem("row_ready")
        turned = sem("turned")
        norm_hi = sem("norm_hi")
        norm_lo = sem("norm_lo")
        scaled_ready = sem("scaled_ready")
        unit_landed = [sem(f"unit_landed{s}") for s in range(LAND)]
        unit_hi = sem("unit_hi")
        unit_lo = sem("unit_lo")
        unit_used = sem("unit_used")
        proj_hi = sem("proj_hi")
        proj_ready = sem("proj_ready")
        gate_ready = sem("gate_ready")
        strip_landed = [sem("strip_landed0"), sem("strip_landed1")]
        strip_masked = sem("strip_masked")
        scores_done = sem("scores_done")
        biased = sem("biased")
        max_ready = sem("max_ready")
        exp_done = sem("exp_done")
        sum_step = sem("sum_step")
        probs_ready = sem("probs_ready")
        pt_done = sem("pt_done")
        pt_hi_done = sem("pt_hi_done")
        pt_lo_done = sem("pt_lo_done")
        pv_done = sem("pv_done")
        att_lo = sem("att_lo")
        att_ready = sem("att_ready")
        at_hi_done = sem("at_hi_done")
        at_lo_done = sem("at_lo_done")
        branch_a = sem("branch_a")
        branch_b = sem("branch_b")
        merged = sem("merged")
        merged_hi = sem("merged_hi")
        merged_lo = sem("merged_lo")
        x2_landed = [sem("x2_landed0"), sem("x2_landed1")]
        gain3_landed = sem("gain3_landed")
        tile_done = sem("tile_done")
        tile_added = sem("tile_added")
        relu_done = sem("relu_done")
        sq_done = sem("sq_done")
        hidden_hi = sem("hidden_hi")
        hidden_lo = sem("hidden_lo")
        left_ready = sem("left_ready")
        right_ready = sem("right_ready")
        stored = sem("stored")

        B2 = UNITS1 // 4
        LOOP2, PER2 = 3, 6
        B2_END = B2 + LOOP2 * PER2
        B3 = B2_END + 2
        B4 = B3 + 8
        N_BLOCKS1 = len(BLOCKS)
        NBR = D // CB

        SQUARED_X = 4 * 2
        FIRST_PAIRS, PAIRS = (4, 6, 0, 2, 0, 2, 4, 6), (0, 2, 4, 6, 0, 2, 4, 6)
        SQUARED_H = 4 * TT
        LAST_GROUPS = ((0, 2), (2, 3), (3, 4))
        ROUND = 4 * (TT - 1)

        WARM_UP = 16
        SPREAD_BANK = 6

        def split_slot(u, kept):
            if kept is not None:
                return (buf[:, 2 * kept:2 * kept + 2, :].rearrange("p k n -> p (k n)") for buf in (at_hi, at_lo))
            return w_hi[:, u % SPLIT, :], w_lo[:, u % SPLIT, :]

        def quad_of(phase3, q):
            return 4 * ((q + 1) % 2) if phase3 else 4 * (q % 2)

        def feature_block(i, second):
            return bank[:, quad_of(True, i // 4) + i % 4, :] if second else feat[:, i, :]

        block = ctx.enter_context(nc.Block())

        @block.sync
        def _(sp):
            def load(b, u, src, width):
                s = u % LAND
                if not (isinstance(b, int) and b == 0):
                    sp.wait_ge(unit_lo, 4 * b + (u - LAND + 1))
                dst = landing[:, s, :].rearrange("p (k n) -> p k n", n=width)
                sp.dma_start(dst, src).then_inc(unit_landed[s], 16)

            def load_block(b, w, col, units=4):
                for u in range(units):
                    load(b, u, w[:, KU * u:KU * (u + 1), bass.ds(col, CB)], CB)

            def strip(h):
                if h >= 2:
                    sp.wait_ge(biased, TT * (h - 1))
                if h < A_HEADS:
                    sp.dma_start(strips[:, h % 2, 0:2 * P], alibi_in[h]).then_inc(strip_landed[h % 2], 16)
                else:
                    if h == A_HEADS:
                        sp.wait_ge(rel_stored, 16)
                    row = bass.AP(rel_rows.tensor, (h - A_HEADS) * REL_ROW, [[1, P], [1, STRIP]])
                    sp.dma_start(strips[:, h % 2, :], row).then_inc(strip_landed[h % 2], 16)

            def load_x(k0, k1, landed):
                sp.dma_start(feat[:, k0:k1, :], x_blocks[:, k0:k1, :]).then_inc(landed, 16)

            load_x(0, 2, x_start_landed)
            n = 0
            for c, (kind, mixer, i) in enumerate(BLOCKS):
                if kind == "g":
                    w, col = wga, (0 if mixer == "a" else D) + i * CB
                else:
                    w, col = win, COL0[kind, mixer] + i * CB
                for u in range(KU):
                    load(c, u, w[:, KU * u:KU * (u + 1), col:col + CB], CB)
                    if c == 0 and u == 0:
                        load_x(2, 4, x_landed[0])
                    if c == 0 and u < 3:
                        load_x(4 * u + 4, 4 * u + 8, x_landed[u + 1])
                    if c == 1:
                        for t in ((0,), (1, 2), (3,), ())[u]:
                            sp.dma_start(x_rows[:, t, :], x_tiles[:, t, :]).then_inc(rows_landed[t], 16)
                    if c == 0 and u == 2:
                        sp.dma_start(rel_table[:, 0:REL + P], b_rel_bias[0, :, REL - P + 1:2 * REL + 1])\
                            .then_inc(rel_landed, 16)
                    if c == 1 and u == 0:
                        sp.dma_start(identity[:], identity_in).then_inc(const_landed, 16)
                        sp.dma_start(sinks[:], a_sinks.rearrange("o k g -> o (k g)").partition_broadcast(P))\
                            .then_inc(sinks_landed, 16)
                    if c == 1 and u == 3:
                        sp.wait_ge(rel_extended, 1)
                        sp.dma_start(rel_rows, rel_table).then_inc(rel_stored, 16)
                        strip(0)
                        strip(1)
                    if n - 6 in SCORES_AT and SCORES_AT.index(n - 6) + 2 < HEADS:
                        strip(SCORES_AT.index(n - 6) + 2)
                    n += 1

            def load_branches(b, nb):
                for u in range(2):
                    load(b, u, wba[:, KU * u:KU * (u + 1), bass.ds(nb * CB, CB)], CB)
                for u in range(2):
                    load(b, 2 + u, wbb[:, KU * u:KU * (u + 1), bass.ds(nb * CB, CB)], CB)

            with sp.Fori(0, LOOP2) as i:
                for j in range(2):
                    b = i * PER2 + (B2 + 3 * j)
                    load_branches(b, i * 2 + j)
                    load_block(b + 1, wga, i * (2 * CB) + (2 + j) * CB)
                    load_block(b + 2, wga, i * (2 * CB) + (D + (2 + j) * CB))
            for j in range(2):
                load_branches(B2_END + j, NBR - 2 + j)

            for q in range(4):
                for u in range(8):
                    cols = slice(q * QC, (q + 1) * QC)
                    load(B3 + 2 * q + u // 4, u % 4, wout[:, 2 * u:2 * u + 2, cols], QC)
                    if u == 5:
                        for r in ((0, 1) if q == 0 else (q + 1,) if q < 3 else ()):
                            if r < 2:
                                sp.wait_ge(merged, NBR)
                            else:
                                sp.wait_ge(tile_added, TT * (r - 1))
                            sp.dma_start(x_again[:, r % 2], x_tiles[:, :, r * QC:(r + 1) * QC])\
                                .then_inc(x2_landed[r % 2], 16)
            def load_up(b, col):
                for j in range(CB_CHUNK):
                    load_block(b + j, wup, col + j * CB)

            def load_down(b, k):
                for q in range(4):
                    for u in range(8):
                        load(b + 2 * q + u // 4, u % 4,
                             wdown[:, bass.ds(k + 2 * u, 2), q * QC:(q + 1) * QC], QC)

            load_up(B4, 0)
            sp.dma_start(gain_row[:], norm_final_g.rearrange("(o d) -> o d", o=1).partition_broadcast(P))\
                .then_inc(gain3_landed, 16)
            with sp.Fori(0, FC - 1) as f:
                load_down(f * 16 + (B4 + 8), f * KB)
                load_up(f * 16 + (B4 + 16), f * D + D)
            last = B4 + 16 * (FC - 1) + 8
            load_down(last, KB * (FC - 1))
            for t in range(TT):
                for half, ready in enumerate((left_ready, right_ready)):
                    sp.wait_ge(ready, t + 1)
                    cols = slice(half * D // 2, (half + 1) * D // 2)
                    sp.dma_start(out_tiles[:, t, cols], x_tok[:, t, cols]).then_inc(stored, 16)
            sp.wait_ge(stored, 16 * 2 * TT)

        @block.scalar
        def _(act):
            def split(b, u, kept=None):
                act.wait_ge(unit_landed[u % LAND], 16 * b + 16)
                if not (isinstance(b, int) and 4 * b + u < SPLIT):
                    act.wait_ge(unit_used, 4 * b + (u - SPLIT + 1))
                hi, _ = split_slot(u, kept)
                nc.scalar.activation(hi, landing[:, u % LAND, :], ACT.Copy).then_inc(unit_hi, 1)

            def norm_block(i, second, x_hi):
                if second:
                    act.wait_ge(turned, i + 1)
                elif i == 0:
                    act.wait_ge(x_start_landed, 16)
                elif i == 2 or i % 4 == 0:
                    act.wait_ge(x_landed[i // 4], 16)
                nc.scalar.activation(x_hi[:, i, :], feature_block(i, second), ACT.Copy,
                                     scale=gains[:, second, i:i + 1]).then_inc(norm_hi, 1)

            def roots(t0, t1, count):
                act.wait_ge(var_ready, count)
                nc.scalar.activation(stat[:, 2, t0:t1], stat[:, 1, t0:t1], ACT.Sqrt).then_inc(root_ready, 1)

            def rms_to_all(count):
                act.wait_ge(row_made, count)
                nc.scalar.activation(rms_row[:], bank[:, SPREAD_BANK, :], ACT.Copy).then_inc(row_ready, 1)

            def evacuate(c):
                kind, mixer, i = BLOCKS[c]
                act.wait_ge(scaled_ready, c + 1)
                if kind == "g":
                    g = gate[:, i, "ab".index(mixer)]
                    nc.scalar.activation(g, g, ACT.Sigmoid).then_inc(gate_ready, 1)
                    return
                if kind == "q":
                    used = last_scores_before_q(mixer, i)
                    if used:
                        act.wait_ge(scores_done, used)
                elif mixer == "b" and i:
                    if kind == "k":
                        act.wait_ge(scores_done, A_HEADS + 4 * (i - 1))
                    else:
                        act.wait_ge(pv_done, A_HEADS + 4 * (i - 1))
                src, hi, _ = block_parts(c)
                nc.scalar.activation(hi, src, ACT.Copy).then_inc(proj_hi, 1)

            def exponentials(h):
                act.wait_ge(max_ready, h + 1)
                if h < A_HEADS:
                    nc.scalar.activation(sink_exp[:], neg_max[:], ACT.Exp, bias=sinks[:, h:h + 1])
                for t, (_, n, _, _, at) in enumerate(head_tiles(h)):
                    nc.scalar.activation(probs[:, at:at + n], probs[:, at:at + n], ACT.Exp,
                                         bias=neg_max[:, t:t + 1], accum_out=row_sum[:, t:t + 1])\
                        .then_inc(exp_done, 1)

            def turned_probs(h):
                for t, (first, n, bk, col, _) in enumerate(head_tiles(h)):
                    act.wait_ge(pt_done, TT * h + bank_end(h, t))
                    nc.scalar.activation(pt_hi[:, t, first * P:first * P + n], bank[:, bk, col:col + n], ACT.Copy)\
                        .then_inc(pt_hi_done, 1)

            def attended(h):
                act.wait_ge(pv_done, h + 1)
                o = (h % 2) * DH
                if h >= 2:
                    act.wait_ge(att_ready, h - 1)
                nc.scalar.activation(from_v_lo[o:o + DH, :], bank[DH:P, PV_BANK, :], ACT.Copy)\
                    .then_inc(att_lo, 1)

            def stage(n):
                if n in PV_AT:
                    attended(PV_AT.index(n))
                if n in SCORES_AT:
                    exponentials(SCORES_AT.index(n))
                if n in TURN_AT:
                    turned_probs(TURN_AT.index(n))
                if n % KU == 0:
                    evacuate(n // KU - 1)

            act.wait_ge(ones_ready, 1)
            nc.scalar.activation(row_sum[:], ones[:, 0:TT], ACT.Copy)
            act.dma_start(gains[:], norm_gains).then_inc(gains_landed, 16)

            act.wait_ge(gains_landed, 16)
            for i in range(KB):
                norm_block(i, 0, xn_hi)
                if i == 0:
                    split(0, 0)
                if i in (3, 7, 11):
                    split(0, i // 4 + 1)
            for t in range(TT):
                if t != 2:
                    split(1, (0, 1, None, 2)[t])
                act.wait_ge(rows_landed[t], 16)
                for g in (0, 1):
                    if t >= 2:
                        act.wait_ge(squared, 2 * t + g - 3)
                    nc.scalar.activation(pt_hi[:, (2 * t + g) % 4, :], x_rows[:, t, g * QC:(g + 1) * QC], ACT.Square,
                                         accum_out=squares[:, t, g:g + 1]).then_inc(squared, 1)
            roots(0, TT, 1)
            split(1, 3)
            rms_to_all(1)
            stage(4)
            act.wait_ge(sinks_landed, 16)

            for n in range(2 * KU, UNITS1):
                split(n // 4, n % 4)
                stage(n - 2)
            split(B2, 0)
            stage(UNITS1 - 2)
            act.wait_ge(scores_done, HEADS)

            def outputs_hi(groups):
                for g in groups:
                    if g == KB // 2 - 1:
                        act.wait_ge(att_ready, HEADS)
                    nc.scalar.activation(at_hi[:, 2 * g:2 * g + 2, :], feat[:, 2 * g:2 * g + 2, :], ACT.Copy)\
                        .then_inc(at_hi_done, 1)

            outputs_hi(range(4))
            split(B2, 1)
            attended(HEADS - 1)
            outputs_hi(range(4, KB // 2))
            evacuate(N_BLOCKS1 - 1)

            def gates(s, m, nb):
                act.wait_ge(scaled_ready, 2 * nb + (m + 1 + N_BLOCKS1 - 4))
                nc.scalar.activation(gate[:, s, m], gate[:, s, m], ACT.Sigmoid).then_inc(gate_ready, 1)

            with act.Fori(0, LOOP2) as i:
                for j in range(2):
                    b = i * PER2 + (B2 + 3 * j)
                    nb = i * 2 + j
                    if j == 1:
                        split(b, 0)
                        split(b, 1)
                        gates(0, 1, nb + 1)
                    split(b, 2)
                    split(b, 3)
                    for u in range(4):
                        split(b + 1, u)
                    split(b + 2, 0)
                    split(b + 2, 1)
                    gates(j, 0, nb + 2)
                    split(b + 2, 2)
                    split(b + 2, 3)
                split(i * PER2 + (B2 + PER2), 0)
                split(i * PER2 + (B2 + PER2), 1)
                gates(1, 1, i * 2 + 3)

            def merged_part(nb):
                act.wait_ge(merged, nb + 1)
                nc.scalar.activation(xn_hi[:, 2 * nb:2 * nb + 2, :], feat[:, 2 * nb:2 * nb + 2, :], ACT.Copy)\
                    .then_inc(merged_hi, 1)

            merged_part(0)
            split(B2_END, 2)
            merged_part(1)
            split(B2_END, 3)
            merged_part(2)
            for u in range(4):
                split(B2_END + 1, u)
                merged_part(3 + u)

            def sum_squares(q, t, final=False):
                unused = at_lo[:, TT * q + t, :]
                if final:
                    unused = side[:, 2048 + t * QC:2048 + (t + 1) * QC]
                    if q:
                        act.wait_ge(squared, SQUARED_X + SQUARED_H + TT * (q - 1) + t + 1)
                nc.scalar.activation(unused, x_tok[:, t, q * QC:(q + 1) * QC], ACT.Square,
                                     accum_out=squares[:, t, q:q + 1]).then_inc(squared, 1)

            def out_quarter(b, first_tile, prev, extra=None):
                for u in range(8):
                    split(b + u // 4, u % 4)
                    if u == 1 and extra is not None:
                        extra()
                    if u == 2 and prev is not None:
                        for t in range(TT):
                            act.wait_ge(tile_added, first_tile + t + 1)
                            sum_squares(prev, t)
                    if u in (5, 6) and prev is not None:
                        for i in (0, 1):
                            norm_block(4 * prev + 2 * (u - 5) + i, 1, at_hi)

            def last_tiles(first_tile, t0, t1, count, final=False):
                for t in range(t0, t1):
                    act.wait_ge(tile_added, first_tile + 3 * TT + t + 1)
                    sum_squares(3, t, final)
                roots(t0, t1, count)

            out_quarter(B3, 0, None, lambda: merged_part(NBR - 1))
            for q in range(1, 4):
                out_quarter(B3 + 2 * q, TT * (q - 1), q - 1)
            split(B4, 0)
            split(B4, 1)
            last_tiles(0, 0, TT, 2)
            split(B4, 2)
            for i in range(KB - 4, KB):
                norm_block(i, 1, at_hi)
            split(B4, 3)
            rms_to_all(2)

            def hidden(j, count):
                act.wait_ge(relu_done, count + 1)
                nc.scalar.activation(xn_hi[:, 2 * j:2 * j + 2, :].rearrange("p b n -> p (b n)"), relu_z, ACT.Square)\
                    .then_inc(hidden_hi, 1)

            def up(b, count, started):
                for j in range(1 if started else 0, CB_CHUNK):
                    for u in range(4):
                        split(b + j, u)
                        if u == 1 and j:
                            hidden(j - 1, count + (j - 1))

            def down(b, count):
                for q in range(4):
                    for u in range(8):
                        split(b + 2 * q + u // 4, u % 4)
                        if q == 0 and u == 1:
                            hidden(CB_CHUNK - 1, count + (CB_CHUNK - 1))

            up(B4, 0, True)
            with act.Fori(0, FC - 1) as f:
                down(f * 16 + (B4 + 8), f * CB_CHUNK)
                up(f * 16 + (B4 + 16), f * CB_CHUNK + CB_CHUNK, False)
            last = B4 + 16 * (FC - 1) + 8
            tiles_before = 4 * TT + 4 * TT * (FC - 1)
            for q in range(4):
                for u in range(8):
                    split(last + 2 * q + u // 4, u % 4, u if q == 3 else None)
                    if q == 0 and u == 1:
                        hidden(CB_CHUNK - 1, CB_CHUNK * FC - 1)
                    if q > 0 and u == 2:
                        for t in range(TT):
                            act.wait_ge(tile_added, tiles_before + TT * (q - 1) + t + 1)
                            sum_squares(q - 1, t, True)
            for group, (t0, t1) in enumerate(LAST_GROUPS):
                last_tiles(tiles_before, t0, t1, 3 + group, True)
                act.wait_ge(inverse_ready, 3 + group)
                act.wait_ge(gained, 3)
                for t in range(t0, t1):
                    left = x_tok[:, t, 0:D // 2]
                    nc.scalar.activation(left, left, ACT.Copy, scale=stat[:, 5, t:t + 1]).then_inc(left_ready, 1)

        @block.vector
        def _(dve):
            steps = [0]

            def step(ins):
                steps[0] += 1
                ins.then_inc(stat_step, 1)
                dve.wait_ge(stat_step, steps[0])

            def split(b, u, kept=None):
                dve.wait_ge(unit_hi, 4 * b + (u + 1))
                hi, lo = split_slot(u, kept)
                nc.vector.tensor_tensor(lo, landing[:, u % LAND, :], hi.bitcast(F32),
                                        ALU.subtract).then_inc(unit_lo, 1)

            def inverse_rms(t0, t1, squares_count, roots_count):
                dve.wait_ge(squared, squares_count)
                total, v, root, r, a, c = (stat[:, k, t0:t1] for k in range(6))
                step(nc.vector.tensor_reduce(total, squares[:, t0:t1, :], AX.X, ALU.add))
                nc.vector.tensor_scalar(v, total, 1.0 / D, EPS, ALU.mult, ALU.add).then_inc(var_ready, 1)
                dve.wait_ge(root_ready, roots_count)
                step(nc.vector.reciprocal(r, root))
                step(nc.vector.tensor_tensor(a, r, r, ALU.mult))
                step(nc.vector.tensor_tensor(c, a, v, ALU.mult))
                step(nc.vector.tensor_scalar(a, c, -0.5, 1.5, ALU.mult, ALU.add))
                nc.vector.tensor_tensor(c, r, a, ALU.mult).then_inc(inverse_ready, 1)
                dve.wait_ge(inverse_ready, roots_count)
                return c

            def to_rows(t_inverse):
                shape = [P, TT, P]
                nc.vector.tensor_tensor(rms_diagonal, identity[:].unsqueeze(1).broadcast_to(shape),
                                        t_inverse.unsqueeze(2).broadcast_to(shape), ALU.mult)\
                    .then_inc(diagonal_ready, 1)

            def norm_block(i, second, x_hi, x_lo):
                dve.wait_ge(norm_hi, KB * second + i + 1)
                nc.vector.scalar_tensor_tensor(out=x_lo[:, i, :], in0=feature_block(i, second),
                                               scalar=gains[:, second, i:i + 1], in1=x_hi[:, i, :].bitcast(F32),
                                               op0=ALU.mult, op1=ALU.subtract).then_inc(norm_lo, 1)

            def by_token(blocks):
                return rms_row[:].unsqueeze(1).broadcast_to([P, blocks, SEQ])

            def scale_block(c):
                kind, mixer, i = BLOCKS[c]
                dve.wait_ge(unit_used, KU * (c + 1))
                if c == 0:
                    dve.wait_ge(row_ready, 1)
                    dve.wait_ge(rel_stored, 16)
                pair = bank[:, 2 * (c % 2):2 * (c % 2) + 2, :]
                if ready_count(c - 1) and (kind != "g" or i == 1):
                    dve.wait_ge(proj_ready, ready_count(c - 1))
                if kind == "g":
                    ins = nc.vector.tensor_tensor(gate[:, i, "ab".index(mixer)], pair, by_token(2), ALU.mult)
                elif kind == "k":
                    ins = nc.vector.tensor_tensor(scaled[:, 0:2, :], pair, by_token(2), ALU.mult)
                elif kind == "v":
                    ins = nc.vector.tensor_tensor(
                        scaled[:, 0:2, :].rearrange("p b (t n) -> p (b t) n", t=2),
                        pair.rearrange("p b (t n) -> p (b t) n", t=2),
                        stat[:, 5, :].unsqueeze(2).broadcast_to([P, TT, CB]), ALU.mult)
                elif mixer == "b":
                    ins = nc.vector.scalar_tensor_tensor(out=scaled[:, 0:2, :], in0=pair, scalar=DH ** -0.5,
                                                         in1=by_token(2), op0=ALU.mult, op1=ALU.mult)
                else:
                    r = (i % 2) * DH
                    for hh in range(4):
                        src = bank[(hh % 2) * DH:(hh % 2 + 1) * DH, 2 * (c % 2) + hh // 2, :]
                        ins = nc.vector.scalar_tensor_tensor(
                            out=scaled[r:r + DH, hh, :], in0=src, scalar=DH ** -0.5,
                            in1=rms_row[r:r + DH, :], op0=ALU.mult, op1=ALU.mult)
                ins.then_inc(scaled_ready, 1)

            def block_lo(c):
                if BLOCKS[c][0] == "g":
                    return
                dve.wait_ge(proj_hi, ready_count(c))
                src, hi, lo = block_parts(c)
                nc.vector.tensor_tensor(lo, src, hi.bitcast(F32), ALU.subtract).then_inc(proj_ready, 1)

            def biased_scores(h):
                s = h % 2
                dve.wait_ge(strip_landed[s], 16 * (h // 2 + 1))
                if h >= A_HEADS:
                    nc.vector.memset(strips[0:CHUNK, s, 0:CHUNK], MASKED).then_inc(strip_masked, 1)
                    dve.wait_ge(strip_masked, h - A_HEADS + 1)
                dve.wait_ge(scores_done, h + 1)
                if h:
                    dve.wait_ge(pt_done, TT * h)
                for t, (_, n, bk, col, at) in enumerate(head_tiles(h)):
                    part = strips[:, s, 0:n]
                    reverse = bass.AP(part.tensor, part.offset + n - 1, [part.ap[0], [-1, n]])
                    nc.vector.tensor_tensor_reduce(
                        out=probs[:, at:at + n], in0=bank[:, bk, col:col + n], in1=reverse, scale=1.0,
                        scalar=LOWEST, op0=ALU.add, op1=ALU.max, accum_out=row_max[:, t:t + 1]).then_inc(biased, 1)
                dve.wait_ge(biased, TT * (h + 1))
                if h < A_HEADS:
                    nc.vector.tensor_scalar(neg_max[:], row_max[:], sinks[:, h:h + 1], -1.0, ALU.max,
                                            ALU.mult).then_inc(max_ready, 1)
                else:
                    nc.vector.tensor_scalar(neg_max[:], row_max[:], -1.0, None, ALU.mult).then_inc(max_ready, 1)

            def attended(h):
                dve.wait_ge(att_lo, h + 1)
                o = (h % 2) * DH
                nc.vector.tensor_tensor(feat[o:o + DH, h // 2, :], bank[0:DH, PV_BANK, :],
                                        from_v_lo[o:o + DH, :], ALU.add).then_inc(att_ready, 1)

            sum_steps = [0]

            def normalise(h):
                dve.wait_ge(exp_done, TT * (h + 1))
                if h < A_HEADS:
                    sum_steps[0] += 1
                    nc.vector.tensor_tensor(row_max[:], row_sum[:], sink_exp[:], ALU.add).then_inc(sum_step, 1)
                    dve.wait_ge(sum_step, sum_steps[0])
                sum_steps[0] += 1
                nc.vector.reciprocal(row_inv[:], row_max[:] if h < A_HEADS else row_sum[:]).then_inc(sum_step, 1)
                dve.wait_ge(sum_step, sum_steps[0])
                for t, (_, n, _, _, at) in enumerate(head_tiles(h)):
                    nc.vector.tensor_scalar(probs[:, at:at + n], probs[:, at:at + n], row_inv[:, t:t + 1], None,
                                            ALU.mult).then_inc(probs_ready, 1)

            def turned_probs(h):
                for t, (first, n, bk, col, _) in enumerate(head_tiles(h)):
                    dve.wait_ge(pt_hi_done, TT * h + bank_end(h, t))
                    nc.vector.tensor_tensor(pt_lo[:, t, first * P:first * P + n], bank[:, bk, col:col + n],
                                            pt_hi[:, t, first * P:first * P + n].bitcast(F32), ALU.subtract)\
                        .then_inc(pt_lo_done, 1)

            nc.vector.memset(ones, 1.0).then_inc(ones_ready, 1)
            dve.wait_ge(gains_landed, 16)
            for i in range(KB):
                if i == 0:
                    dve.wait_ge(x_start_landed, 16)
                elif i == 2 or i % 4 == 0:
                    dve.wait_ge(x_landed[i // 4], 16)
                norm_block(i, 0, xn_hi, xn_lo)
                if i == 0:
                    split(0, 0)
                if i in (3, 7, 11):
                    split(0, i // 4 + 1)
            dve.wait_ge(rel_landed, 16)
            last = REL + P
            nc.vector.tensor_copy(rel_table[:, last:REL_ROW],
                                  rel_table[:, last - 1:last].broadcast_to([B_HEADS, REL_ROW - last]))\
                .then_inc(rel_extended, 1)
            for t in range(TT):
                if t != 2:
                    split(1, (0, 1, None, 2)[t])
                dve.wait_ge(rows_landed[t], 16)
                for g in (2, 3):
                    if t >= 1:
                        dve.wait_ge(others_squared, 2 * t + g - 3)
                    part = x_rows[:, t, g * QC:(g + 1) * QC]
                    nc.vector.tensor_tensor_reduce(
                        out=probs[:, (g - 2) * QC:(g - 1) * QC], in0=part, in1=part, scale=1.0, scalar=0.0,
                        op0=ALU.mult, op1=ALU.add, accum_out=squares[:, t, g:g + 1]).then_inc(others_squared, 1)
            dve.wait_ge(others_squared, 2 * TT)
            dve.wait_ge(sinks_landed, 16)
            dve.wait_ge(const_landed, 16)
            to_rows(inverse_rms(0, TT, SQUARED_X, 1))
            split(1, 3)
            scale_block(0)
            block_lo(0)

            for n in range(2 * KU, UNITS1 + 1):
                m = n - 2
                head = SCORES_AT.index(m) if m in SCORES_AT else None
                if head is not None:
                    biased_scores(head)
                split(n // 4, n % 4)
                if m in TURN_AT:
                    turned_probs(TURN_AT.index(m))
                if m in PV_AT:
                    attended(PV_AT.index(m))
                if head is not None:
                    normalise(head)
                if m % KU == KU - 1:
                    scale_block(m // KU)
                if m % KU == 0:
                    block_lo(m // KU - 1)
            for g in range(KB // 2):
                if g == 0:
                    dve.wait_ge(pv_done, HEADS - 4)
                if g == 2:
                    split(B2, 1)
                    dve.wait_ge(pv_done, HEADS)
                if g == 4:
                    attended(HEADS - 1)
                    scale_block(N_BLOCKS1 - 1)
                dve.wait_ge(at_hi_done, g + 1)
                nc.vector.tensor_tensor(at_lo[:, 2 * g:2 * g + 2, :], feat[:, 2 * g:2 * g + 2, :],
                                        at_hi[:, 2 * g:2 * g + 2, :].bitcast(F32), ALU.subtract)\
                    .then_inc(at_lo_done, 1)

            def scaled_a(b, s, nb):
                dve.wait_ge(unit_used, 4 * b + 2)
                dve.wait_ge(gate_ready, 2 * nb + 2)
                nc.vector.tensor_tensor(feat[:, bass.ds(2 * nb, 2), :], gate[:, s, 0], bank[:, 0:2, :], ALU.mult)\
                    .then_inc(branch_a, 1)

            def merge_b(b, s, nb):
                dve.wait_ge(unit_used, 4 * b + 4)
                nc.vector.tensor_tensor(gate[:, s, 1], gate[:, s, 1], bank[:, 2:4, :], ALU.mult)\
                    .then_inc(branch_b, 1)
                dve.wait_ge(branch_a, nb + 1)
                dve.wait_ge(branch_b, nb + 1)
                nc.vector.tensor_tensor(feat[:, bass.ds(2 * nb, 2), :], feat[:, bass.ds(2 * nb, 2), :],
                                        gate[:, s, 1], ALU.add).then_inc(merged, 1)

            def gate_logits(b, s, m, nb):
                dve.wait_ge(unit_used, 4 * b + 4)
                dve.wait_ge(merged, nb - 1)
                nc.vector.tensor_tensor(gate[:, s, m], bank[:, 2 * m:2 * m + 2, :], by_token(2), ALU.mult)\
                    .then_inc(scaled_ready, 1)

            with dve.Fori(0, LOOP2) as i:
                for j in range(2):
                    b = i * PER2 + (B2 + 3 * j)
                    nb = i * 2 + j
                    if j == 1:
                        split(b, 0)
                        split(b, 1)
                        gate_logits(b - 1, 0, 1, nb + 1)
                    split(b, 2)
                    split(b, 3)
                    scaled_a(b, j, nb)
                    split(b + 1, 0)
                    split(b + 1, 1)
                    merge_b(b, j, nb)
                    split(b + 1, 2)
                    split(b + 1, 3)
                    split(b + 2, 0)
                    split(b + 2, 1)
                    gate_logits(b + 1, j, 0, nb + 2)
                    split(b + 2, 2)
                    split(b + 2, 3)
                split(i * PER2 + (B2 + PER2), 0)
                split(i * PER2 + (B2 + PER2), 1)
                gate_logits(i * PER2 + (B2 + PER2 - 1), 1, 1, i * 2 + 3)

            def merged_part(nb):
                dve.wait_ge(merged_hi, nb + 1)
                nc.vector.tensor_tensor(xn_lo[:, 2 * nb:2 * nb + 2, :], feat[:, 2 * nb:2 * nb + 2, :],
                                        xn_hi[:, 2 * nb:2 * nb + 2, :].bitcast(F32), ALU.subtract)\
                    .then_inc(merged_lo, 1)

            merged_part(0)
            split(B2_END, 2)
            merged_part(1)
            split(B2_END, 3)
            scaled_a(B2_END, 0, NBR - 2)
            merged_part(2)
            for u in range(4):
                split(B2_END + 1, u)
                if u == 1:
                    merge_b(B2_END, 0, NBR - 2)
                if u == 3:
                    scaled_a(B2_END + 1, 1, NBR - 1)
                merged_part(3 + u)

            def tile_complete(k, tiles, before, b):
                if k < tiles - 1:
                    dve.wait_ge(tile_done, before + (k + 1))
                else:
                    dve.wait_ge(unit_used, 4 * b + 8)

            def residual(q, t, before, b):
                tile_complete(t, TT, before, b)
                add_tile(q, t)

            def add_tile(q, t):
                dst = x_tok[:, t, q * QC:(q + 1) * QC]
                nc.vector.tensor_tensor(dst, dst, bank[:, quad_of(False, q) + t, :], ALU.add)\
                    .then_inc(tile_added, 1)

            def residual3(q):
                dve.wait_ge(x2_landed[q % 2], 16 * (q // 2 + 1))
                for t in range(TT):
                    tile_complete(t, TT, (TT - 1) * q, B3 + 2 * q)
                    nc.vector.tensor_tensor(x_tok[:, t, q * QC:(q + 1) * QC], x_again[:, q % 2, t, :],
                                            bank[:, quad_of(True, q) + t, :], ALU.add).then_inc(tile_added, 1)

            for q in range(4):
                for u in range(8):
                    split(B3 + 2 * q + u // 4, u % 4)
                    if q == 0 and u == 1:
                        merge_b(B2_END + 1, 1, NBR - 1)
                        merged_part(NBR - 1)
                    if q > 0 and u == 1:
                        residual3(q - 1)
                    if q > 0 and u in (5, 6):
                        for i in (0, 1):
                            norm_block(4 * (q - 1) + 2 * (u - 5) + i, 1, at_hi, at_lo)

            split(B4, 0)
            split(B4, 1)
            residual3(3)
            dve.wait_ge(tile_added, 4 * TT)
            nc.vector.memset(ones, 1.0).then_inc(ones_ready, 1)
            to_rows(inverse_rms(0, TT, SQUARED_X + SQUARED_H, 2))
            split(B4, 2)
            for i in range(KB - 4, KB):
                norm_block(i, 1, at_hi, at_lo)
            split(B4, 3)

            def hidden(b, j, pair, count):
                dve.wait_ge(unit_used, 4 * b + 4)
                if j == 0:
                    dve.wait_ge(row_ready, 2)
                relu_pair, square_pair = (buf.rearrange("p (b n) -> p b n", b=2) for buf in (relu_z, relu_sq))
                nc.vector.scalar_tensor_tensor(out=relu_pair, in0=bank[:, pair:pair + 2, :], scalar=0.0,
                                               in1=by_token(2), op0=ALU.max, op1=ALU.mult).then_inc(relu_done, 1)
                dve.wait_ge(relu_done, count + 1)
                nc.vector.tensor_tensor(square_pair, relu_pair, relu_pair, ALU.mult).then_inc(sq_done, 1)
                dve.wait_ge(sq_done, count + 1)
                dve.wait_ge(hidden_hi, count + 1)
                nc.vector.tensor_tensor(xn_lo[:, 2 * j:2 * j + 2, :], square_pair,
                                        xn_hi[:, 2 * j:2 * j + 2, :].bitcast(F32), ALU.subtract)\
                    .then_inc(hidden_lo, 1)

            def up(b, count, started, before):
                for j in range(1 if started else 0, CB_CHUNK):
                    for u in range(4):
                        split(b + j, u)
                        if u == 1 and j:
                            hidden(b + j - 1, j - 1, (FIRST_PAIRS if started else PAIRS)[j - 1], count + (j - 1))
                        if u == 1 and not j and before is not None:
                            for t in range(TT):
                                residual(3, t, before + 3 * (TT - 1), b - 2)

            def times_gain(q):
                dve.wait_ge(squared, SQUARED_X + SQUARED_H + TT * (q + 1))
                h = x_tok[:, :, q * QC:(q + 1) * QC]
                gain = gain_row[:, q * QC:(q + 1) * QC].unsqueeze(1).broadcast_to([P, TT, QC])
                nc.vector.tensor_tensor(h, h, gain, ALU.mult).then_inc(gained, 1)

            def down(b, count, before, final=False):
                for q in range(4):
                    for u in range(8):
                        split(b + 2 * q + u // 4, u % 4, u if final and q == 3 else None)
                        if final and q > 0 and u == 4:
                            times_gain(q - 1)
                        if q == 0 and u == 1:
                            hidden(b - 1, CB_CHUNK - 1, 6, count + (CB_CHUNK - 1))
                        if q > 0 and u == 1:
                            for t in range(TT):
                                residual(q - 1, t, before + (TT - 1) * (q - 1), b + 2 * (q - 1))

            up(B4, 0, True, None)
            with dve.Fori(0, FC - 1) as f:
                down(f * 16 + (B4 + 8), f * CB_CHUNK, f * ROUND + ROUND)
                up(f * 16 + (B4 + 16), f * CB_CHUNK + CB_CHUNK, False, f * ROUND + ROUND)
            last = B4 + 16 * (FC - 1) + 8
            before = ROUND * FC
            dve.wait_ge(gain3_landed, 16)
            down(last, CB_CHUNK * (FC - 1), before, True)
            for group, (t0, t1) in enumerate(LAST_GROUPS):
                for t in range(t0, t1):
                    if group == 0 and t == t1 - 1:
                        dve.wait_ge(unit_used, 4 * (last + 8))
                    else:
                        dve.wait_ge(tile_done, before + 3 * (TT - 1) + (t + 1 if group == 0 else group + 1))
                    add_tile(3, t)
                inverse_rms(t0, t1, SQUARED_X + SQUARED_H + 12 + t1, 3 + group)
                for t in range(t0, t1):
                    c = stat[:, 5, t:t + 1]
                    if t == 0:
                        dve.wait_ge(gained, 3)
                    nc.vector.tensor_scalar(x_tok[:, t, D // 2:3 * QC], x_tok[:, t, D // 2:3 * QC], c, None, ALU.mult)
                    nc.vector.scalar_tensor_tensor(out=x_tok[:, t, 3 * QC:], in0=x_tok[:, t, 3 * QC:], scalar=c,
                                                   in1=gain_row[:, 3 * QC:], op0=ALU.mult, op1=ALU.mult)\
                        .then_inc(right_ready, 1)

        @block.tensor
        def _(pe):
            def product(dst, a_hi, a_lo, b_hi, b_lo, start, stop, **kw):
                nc.tensor.matmul(dst, a_hi, b_hi, start=start, stop=False, **kw)
                nc.tensor.matmul(dst, a_hi, b_lo, start=False, stop=False, **kw)
                return nc.tensor.matmul(dst, a_lo, b_hi, start=False, stop=stop, **kw)

            def turn(i):
                for t in range(TT):
                    ins = nc.tensor.transpose(bank[:, quad_of(True, i // 4) + i % 4, t * P:(t + 1) * P],
                                              x_tok[:, t, i * P:(i + 1) * P], identity[:])
                ins.then_inc(turned, 1)

            def spread_rms(second):
                pe.wait_ge(ones_ready, second + 1)
                pe.wait_ge(diagonal_ready, second + 1)
                nc.tensor.matmul(bank[:, SPREAD_BANK, :], ones, rms_diagonal.rearrange("p t n -> p (t n)"),
                                 start=True, stop=True).then_inc(row_made, 1)

            def first_block():
                for u in range(KU):
                    pe.wait_ge(unit_lo, u + 1)
                    s = u % SPLIT
                    wh = w_hi[:, s, :].rearrange("p (k n) -> p k n", n=CB)
                    wl = w_lo[:, s, :].rearrange("p (k n) -> p k n", n=CB)
                    for k in range(KU):
                        i = KU * u + k
                        pe.wait_ge(norm_lo, i + 1)
                        for nb in range(2):
                            cols = slice(nb * P, (nb + 1) * P)
                            ins = product(bank[:, nb, :], wh[:, k, cols], wl[:, k, cols], xn_hi[:, i, :],
                                          xn_lo[:, i, :], i == 0, i == KB - 1)
                    ins.then_inc(unit_used, 1)

            def features(b, u, pair, k0, first, last, x_hi, x_lo):
                pe.wait_ge(unit_lo, 4 * b + (u + 1))
                s = u % SPLIT
                wh = w_hi[:, s, :].rearrange("p (k n) -> p k n", n=CB)
                wl = w_lo[:, s, :].rearrange("p (k n) -> p k n", n=CB)
                for nb in range(2):
                    for k in range(KU):
                        cols = slice(nb * P, (nb + 1) * P)
                        ins = product(bank[:, pair + nb, :], wh[:, k, cols], wl[:, k, cols],
                                      x_hi[:, k0 + k, :], x_lo[:, k0 + k, :],
                                      first and k == 0, last and k == KU - 1)
                ins.then_inc(unit_used, 1)

            def values(b, u, pair):
                pe.wait_ge(unit_lo, 4 * b + (u + 1))
                s = u % SPLIT
                wh = w_hi[:, s, :].rearrange("p (k n) -> p k n", n=CB)
                wl = w_lo[:, s, :].rearrange("p (k n) -> p k n", n=CB)
                for k in range(KU):
                    for t in range(TT):
                        cols = slice(t * P, (t + 1) * P)
                        kb = KU * u + k
                        dst = bank[:, pair + t // 2, (t % 2) * CB:(t % 2 + 1) * CB]
                        ins = product(dst, xn_hi[:, kb, cols], xn_lo[:, kb, cols], wh[:, k, :], wl[:, k, :],
                                      kb == 0 and t % 2 == 0, kb == KB - 1, skip_group_check=True)
                ins.then_inc(unit_used, 1)

            def scores(h):
                mixer, g = ("a", h // 4) if h < A_HEADS else ("b", (h - A_HEADS) // 4)
                hh = h % 4
                if h:
                    pe.wait_ge(pt_lo_done, TT * h)
                pe.wait_ge(proj_ready, max(ready_count(block_no(kind, mixer, g if kind == "q" or mixer == "b" else 0))
                                           for kind in "qk"))
                if mixer == "a":
                    r, qb, kb = (g % 2) * DH, hh, g // 2
                else:
                    r, qb, kb = (hh % 2) * DH, 2 * (g % 2) + hh // 2, hh // 2
                s = slot_of(mixer, g)
                for t, (first, n, bk, col, _) in enumerate(head_tiles(h)):
                    qs, ks = slice(t * P, (t + 1) * P), slice(first * P, first * P + n)
                    ins = product(bank[:, bk, col:col + n], q_hi[r:r + DH, qb, qs], q_lo[r:r + DH, qb, qs],
                                  k_hi[r:r + DH, s, kb, ks], k_lo[r:r + DH, s, kb, ks], True, True)
                ins.then_inc(scores_done, 1)

            def turn_probs(h):
                if h == 0:
                    pe.wait_ge(const_landed, 16)
                for t, (_, n, bk, col, at) in enumerate(head_tiles(h)):
                    pe.wait_ge(probs_ready, TT * h + t + 1)
                    for k in range(n // P):
                        ins = nc.tensor.transpose(bank[:, bk, col + k * P:col + (k + 1) * P],
                                                  probs[:, at + k * P:at + (k + 1) * P], identity[:])
                    ins.then_inc(pt_done, 1)

            def times_v(h):
                mixer, g = ("a", 0) if h < A_HEADS else ("b", (h - A_HEADS) // 4)
                head = h // 4 if h < A_HEADS else h % 4
                s = slot_of(mixer, g)
                pe.wait_ge(proj_ready, ready_count(block_no("v", mixer, g)))
                pe.wait_ge(pt_lo_done, TT * (h + 1))
                if h:
                    pe.wait_ge(att_ready, h)
                for j in range(TT):
                    last = min(j + 2, TT) if h < A_HEADS else TT
                    dst = bank[:, PV_BANK, j * P:last * P].rearrange("p (t q) -> p t q", q=P)
                    for part in (pt_hi, pt_lo):
                        ins = nc.tensor.matmul(dst, v_parts[:, s, j, head, :],
                                               part[:, j:last, j * P:(j + 1) * P],
                                               start=j == 0 and part is pt_hi,
                                               stop=j == TT - 1 and part is pt_lo, skip_group_check=True)
                ins.then_inc(pv_done, 1)

            pe.wait_ge(ones_ready, 1)
            for _ in range(WARM_UP):
                nc.tensor.matmul(bank[:, SPREAD_BANK, 0:P], ones, ones, start=True, stop=True)
            first_block()

            for n in range(KU, UNITS1):
                c, u = n // KU, n % KU
                kind, _, _ = BLOCKS[c]
                if u == 0 and c >= 2:
                    pe.wait_ge(scaled_ready, c - 1)
                if kind == "v":
                    values(c, u, 2 * (c % 2))
                else:
                    features(c, u, 2 * (c % 2), KU * u, u == 0, u == KU - 1, xn_hi, xn_lo)
                if n == KU + 2:
                    spread_rms(0)
                if n in PV_AT:
                    times_v(PV_AT.index(n))
                if n in SCORES_AT:
                    scores(SCORES_AT.index(n))
                if n in TURN_AT:
                    turn_probs(TURN_AT.index(n))

            def branches(b, nb):
                pe.wait_ge(scaled_ready, 2 * nb + (N_BLOCKS1 - 1))
                for u in range(2):
                    pe.wait_ge(at_lo_done, 2 * u + 2)
                    features(b, u, 0, KU * u, u == 0, u == 1, at_hi, at_lo)
                pe.wait_ge(scaled_ready, 2 * nb + N_BLOCKS1)
                for u in range(2):
                    pe.wait_ge(at_lo_done, 2 * u + 6)
                    features(b, 2 + u, 2, KB // 2 + KU * u, u == 0, u == 1, at_hi, at_lo)

            def gate_block(b, pair, left):
                pe.wait_ge(branch_b if pair else branch_a, left)
                for u in range(4):
                    features(b, u, 2 * pair, KU * u, u == 0, u == 3, xn_hi, xn_lo)

            with pe.Fori(0, LOOP2) as i:
                for j in range(2):
                    b = i * PER2 + (B2 + 3 * j)
                    nb = i * 2 + j
                    branches(b, nb)
                    gate_block(b + 1, 0, nb + 1)
                    gate_block(b + 2, 1, nb + 1)
            branches(B2_END, NBR - 2)
            pe.wait_ge(branch_a, NBR - 1)
            for u in range(2):
                features(B2_END + 1, u, 0, KU * u, u == 0, u == 1, at_hi, at_lo)
            pe.wait_ge(branch_b, NBR - 1)
            for u in range(2):
                features(B2_END + 1, 2 + u, 2, KB // 2 + KU * u, u == 0, u == 1, at_hi, at_lo)

            def quarter(b, first_bank, before, x_hi, x_lo, ready=None, tiles=range(TT), after=None, kept=False):
                for u in range(8):
                    pe.wait_ge(unit_lo, 4 * b + (u + 1))
                    wh, wl = (part.rearrange("p (k n) -> p k n", n=QC) for part in split_slot(u, u if kept else None))
                    if ready is not None:
                        ready(u)
                    for k in range(2):
                        kb = 2 * u + k
                        for t in tiles:
                            if kb == 0:
                                before(t)
                            cols = slice(t * P, (t + 1) * P)
                            ins = product(bank[:, first_bank + t, :], x_hi[:, kb, cols], x_lo[:, kb, cols],
                                          wh[:, k, :], wl[:, k, :], kb == 0, kb == KB - 1)
                            if kb == KB - 1 and t != tiles[-1]:
                                ins.then_inc(tile_done, 1)
                    ins.then_inc(unit_used, 1)
                    if after is not None:
                        after(u)

            def before3(q):
                def wait(t):
                    if q == 0 and t == 0:
                        pe.wait_ge(att_ready, HEADS)
                    if q == 1 and t == 0:
                        pe.wait_ge(branch_b, NBR)
                    if q >= 2:
                        pe.wait_ge(norm_lo, KB + 4 * (q - 2) + t + 1)
                return wait

            def turn_quarter(q):
                pe.wait_ge(tile_added, TT * (q + 1))
                for i in range(4 * q, 4 * q + 4):
                    turn(i)

            for q in range(4):
                quarter(B3 + 2 * q, quad_of(True, q), before3(q), xn_hi, xn_lo,
                        (lambda u: pe.wait_ge(merged_lo, u + 1)) if q == 0 else None,
                        after=(lambda u, q=q: turn_quarter(q - 1) if u == 3 else None) if q else None)
            for u in range(KU):
                pe.wait_ge(norm_lo, KB + KU * (u + 1))
                if u == 0:
                    pe.wait_ge(norm_lo, KB + 10)
                features(B4, u, FIRST_PAIRS[0], KU * u, u == 0, u == 3, at_hi, at_lo)
                if u == 0:
                    turn_quarter(3)
                if u == 1:
                    pe.wait_ge(norm_lo, KB + 12)
                    spread_rms(1)

            def up(b, count, tiles):
                for j in range(0 if tiles is not None else 1, CB_CHUNK):
                    if tiles is None and j >= 4:
                        pe.wait_ge(relu_done, (3, 4, 1, 2)[j - 4])
                    elif j >= 4:
                        pe.wait_ge(relu_done, count + (j - 3))
                    elif tiles is not None:
                        pe.wait_ge(tile_added, tiles + 2 * TT + 2 * j + 2)
                    elif j == 1:
                        pe.wait_ge(row_ready, 2)
                    for u in range(4):
                        pair = (PAIRS if tiles is not None else FIRST_PAIRS)[j]
                        features(b + j, u, pair, KU * u, u == 0, u == 3, at_hi, at_lo)

            def down(b, count, tiles, quarters=range(4)):
                for q in quarters:
                    def before(t, q=q):
                        if q < 2 and t % 2 == 0:
                            pe.wait_ge(relu_done, count + (5 + 2 * q + t // 2))
                        if q >= 2:
                            pe.wait_ge(tile_added, tiles + (TT * (q - 2) + t + 1))

                    def ready(u):
                        pe.wait_ge(hidden_lo, count + (u + 1))

                    quarter(b + 2 * q, quad_of(False, q), before, xn_hi, xn_lo, ready if q == 0 else None)

            up(B4, 0, None)
            with pe.Fori(0, FC - 1) as f:
                tiles = f * (4 * TT) + 4 * TT
                down(f * 16 + (B4 + 8), f * CB_CHUNK, tiles)
                up(f * 16 + (B4 + 16), f * CB_CHUNK + CB_CHUNK, tiles)
            last = B4 + 16 * (FC - 1) + 8
            down(last, CB_CHUNK * (FC - 1), 4 * TT * FC, range(3))

            def before_last(t):
                pe.wait_ge(tile_added, 4 * TT * FC + TT + t + 1)

            quarter(last + 6, quad_of(False, 3), before_last, xn_hi, xn_lo, None, (0, 1), kept=True)
            for t in (2, 3):
                before_last(t)
                for kb in range(KB):
                    ins = product(bank[:, quad_of(False, 3) + t, :], xn_hi[:, kb, t * P:(t + 1) * P],
                                  xn_lo[:, kb, t * P:(t + 1) * P], at_hi[:, kb, :], at_lo[:, kb, :],
                                  kb == 0, kb == KB - 1)
                ins.then_inc(tile_done, 1)


def last_scores_before_q(mixer, i):
    if mixer == "a":
        return 4 * (i - 1) if i >= 2 else 0
    return A_HEADS if i == 0 else A_HEADS if i == 1 else A_HEADS + 4 * (i - 1)


_INS = ["x", "w_in", "a_sinks", "b_rel_bias", "w_branch_a", "w_branch_b", "w_gate",
        "w_out", "w_mlp_in", "w_mlp_out", "norm_final_g"]


def alibi_strips():
    slopes = (2.0 ** (-8.0 * np.arange(1, A_HEADS + 1) / A_HEADS)).astype(np.float32)
    r, v = np.arange(P)[:, None], np.arange(2 * P)[None, :]
    dist = np.abs(r + v - (P - 1)).astype(np.float32)
    key_chunk = (2 * P - 1 - v) // CHUNK
    query_chunk = 2 + r // CHUNK
    seen = (key_chunk <= query_chunk) & (key_chunk >= query_chunk - 1)
    return np.where(seen[None], -slopes[:, None, None] * dist[None], np.float32(MASKED)).astype(np.float32)


def kernel(**inputs):
    import concourse.bacc as _bacc
    from concourse import mybir as _mybir
    from concourse.bass_utils import run_bass_kernel_spmd as _run

    nc = _bacc.Bacc("TRN2", target_bir_lowering=False, num_devices=1, dynamic_dma_scratch_size=1024)
    arrays, args = {}, []
    norm_gains = np.stack([inputs[name].reshape(KB, P).T for name in ("norm_mix_g", "norm_mlp_g")], axis=1)
    others = {"x_features": inputs["x"][0].T, "norm_gains": norm_gains,
              "identity": np.eye(P, dtype=np.float32), "alibi": alibi_strips()}
    for name in [*_INS, *others]:
        a = np.ascontiguousarray(others[name] if name in others else inputs[name])
        arrays[f"in_{name}"] = a
        args.append(nc.dram_tensor(f"in_{name}", a.shape, _mybir.dt.from_np(a.dtype), kind="ExternalInput").ap())
    args.append(nc.dram_tensor("out_0", (1, SEQ, D), F32, kind="ExternalOutput").ap())
    build(nc, *args)
    r = _run(nc, [arrays], core_ids=[0])
    return r.results[0]["out_0"]
```
